# Optimizing a Trainium2 kernel written in Bass

```python
import math
import jax, jax.numpy as jnp
from jax import lax
import numpy as np

D_MODEL = 2048
BATCH = 1
SEQ = 256
DEPTH = 2

N_MIXERS = 2
BLOCK = 128
A_HEADS = 32
A_KV_HEADS = 4
A_HEAD_DIM = 64
A_GROUP = A_HEADS // A_KV_HEADS
WINDOW = 128
A_QKV_DIM = (A_HEADS + 2 * A_KV_HEADS) * A_HEAD_DIM
B_HEADS = 16
B_HEAD_DIM = 64
B_V_DIM = 2 * B_HEAD_DIM
B_QKV_DIM = B_HEADS * (2 * B_HEAD_DIM + 2 * B_HEAD_DIM + B_V_DIM)
P_HEADS = 8
N_KEYS = 128
N_EXPERTS = N_KEYS * N_KEYS
P_TOPK = 16
P_KEY_DIM = 256
P_HALF = P_KEY_DIM // 2
P_CHUNK = 128

LN_EPS = 1e-5
NEG = -1e30
ALPHA = (2.0 * DEPTH) ** 0.25
BETA = (8.0 * DEPTH) ** -0.25
N_A_LAYERS = (DEPTH + 1) // 2
N_B_LAYERS = DEPTH // 2

kernel_name = "hybrid_swa_sink_diffattn_peer_deepnorm"

def alibi_slopes(n):
    return jnp.asarray((2.0 ** (-8.0 * np.arange(1, n + 1) / n)).astype(np.float32))

def layer_norm(x, g, b):
    xf = x.astype(jnp.float32)
    mu = jnp.mean(xf, axis=-1, keepdims=True)
    var = jnp.mean(jnp.square(xf - mu), axis=-1, keepdims=True)
    y = (xf - mu) * lax.rsqrt(var + LN_EPS)
    return (y * g.astype(jnp.float32) + b.astype(jnp.float32)).astype(x.dtype)

def sliding_window_gqa(x, w_qkv, sinks, w_o):
    B, S, _ = x.shape
    nb = S // BLOCK
    d = A_HEAD_DIM
    qkv = x @ w_qkv
    q, k, v = jnp.split(qkv, [A_HEADS * d, (A_HEADS + A_KV_HEADS) * d], axis=-1)
    q = q.reshape(B, nb, BLOCK, A_KV_HEADS, A_GROUP, d)
    k = k.reshape(B, S, A_KV_HEADS, d)
    v = v.reshape(B, S, A_KV_HEADS, d)
    pad = jnp.zeros((B, BLOCK, A_KV_HEADS, d), x.dtype)
    kp = jnp.concatenate([pad, k], axis=1).reshape(B, nb + 1, BLOCK, A_KV_HEADS, d)
    vp = jnp.concatenate([pad, v], axis=1).reshape(B, nb + 1, BLOCK, A_KV_HEADS, d)
    k_band = jnp.concatenate([kp[:, :-1], kp[:, 1:]], axis=2)
    v_band = jnp.concatenate([vp[:, :-1], vp[:, 1:]], axis=2)

    scores = jnp.einsum('bnqhgd,bnkhd->bnhgqk', q, k_band).astype(jnp.float32) * (d ** -0.5)
    qpos = jnp.arange(BLOCK)[:, None] + BLOCK
    kpos = jnp.arange(2 * BLOCK)[None, :]
    dist = qpos - kpos
    blk = jnp.arange(nb)[:, None, None]
    key_abs = (blk - 1) * BLOCK + kpos[None]
    valid = (dist[None] >= 0) & (dist[None] < WINDOW) & (key_abs >= 0)
    slopes = alibi_slopes(A_HEADS).reshape(A_KV_HEADS, A_GROUP)
    scores = scores - slopes[:, :, None, None] * dist.astype(jnp.float32)
    scores = jnp.where(valid[None, :, None, None], scores, NEG)

    sink = sinks.astype(jnp.float32).reshape(A_KV_HEADS, A_GROUP)[:, :, None, None]
    m = jnp.maximum(jnp.max(scores, axis=-1, keepdims=True), sink)
    p = jnp.exp(scores - m)
    denom = jnp.sum(p, axis=-1, keepdims=True) + jnp.exp(sink - m)
    probs = (p / denom).astype(x.dtype)
    o = jnp.einsum('bnhgqk,bnkhd->bnqhgd', probs, v_band)
    return o.reshape(B, S, A_HEADS * d) @ w_o

def differential_attention(x, w_qkv, lq1, lk1, lq2, lk2, subln_g, w_o, lambda_init):
    B, S, _ = x.shape
    nb = S // BLOCK
    d = B_HEAD_DIM
    qkv = x @ w_qkv
    q, k, v = jnp.split(qkv, 3, axis=-1)
    q = q.reshape(B, S, B_HEADS, 2, d)
    k = k.reshape(B, S, B_HEADS, 2, d)
    v = v.reshape(B, S, B_HEADS, B_V_DIM)
    lam = (jnp.exp(jnp.sum(lq1.astype(jnp.float32) * lk1.astype(jnp.float32)))
           - jnp.exp(jnp.sum(lq2.astype(jnp.float32) * lk2.astype(jnp.float32)))
           + lambda_init)
    slopes = alibi_slopes(B_HEADS)[None, :, None, None, None]
    kpos = jnp.arange(S)

    def block(i):
        qb = lax.dynamic_slice_in_dim(q, i * BLOCK, BLOCK, axis=1)
        s = jnp.einsum('bqhcd,bkhcd->bhcqk', qb, k).astype(jnp.float32) * (d ** -0.5)
        qpos = i * BLOCK + jnp.arange(BLOCK)
        dist = qpos[:, None] - kpos[None, :]
        s = s - slopes * dist.astype(jnp.float32)
        s = jnp.where(dist >= 0, s, NEG)
        p = jax.nn.softmax(s, axis=-1)
        pdiff = (p[:, :, 0] - lam * p[:, :, 1]).astype(x.dtype)
        return jnp.einsum('bhqk,bkhe->bqhe', pdiff, v)

    o = lax.map(block, jnp.arange(nb))
    o = o.transpose(1, 0, 2, 3, 4).reshape(B, S, B_HEADS, B_V_DIM)
    of = o.astype(jnp.float32)
    of = of * lax.rsqrt(jnp.mean(jnp.square(of), axis=-1, keepdims=True) + LN_EPS)
    of = of * subln_g.astype(jnp.float32) * (1.0 - lambda_init)
    return of.astype(x.dtype).reshape(B, S, B_HEADS * B_V_DIM) @ w_o

def peer_ffn(x, w_q, subkeys, u, v):
    B, S, D = x.shape
    xt = x.reshape(B * S // P_CHUNK, P_CHUNK, D)

    def chunk(xc):
        T = xc.shape[0]
        q = (xc @ w_q).reshape(T, P_HEADS, 2, P_HALF)
        sc = jnp.einsum('thcd,hckd->thck', q, subkeys).astype(jnp.float32)
        s_top, i_top = lax.top_k(sc, P_TOPK)
        cand = s_top[:, :, 0, :, None] + s_top[:, :, 1, None, :]
        cand_idx = i_top[:, :, 0, :, None] * N_KEYS + i_top[:, :, 1, None, :]
        cand = cand.reshape(T, P_HEADS, P_TOPK * P_TOPK)
        cand_idx = cand_idx.reshape(T, P_HEADS, P_TOPK * P_TOPK)
        best, pos = lax.top_k(cand, P_TOPK)
        experts = jnp.take_along_axis(cand_idx, pos, axis=-1)
        g = jax.nn.softmax(best, axis=-1).reshape(T, P_HEADS * P_TOPK)
        e = experts.reshape(T, P_HEADS * P_TOPK)
        ue = u[e]
        ve = v[e]
        act = jax.nn.gelu(jnp.einsum('ted,td->te', ue, xc).astype(jnp.float32), approximate=False)
        h = (g * act).astype(x.dtype)
        return jnp.einsum('te,ted->td', h, ve)

    return lax.map(chunk, xt).reshape(B, S, D)

def setup_inputs(seed: int = 0) -> dict:
    key = jax.random.key(seed)
    ks = jax.random.split(key, 20)
    f32 = jnp.float32
    D = D_MODEL
    nrm = lambda k, shape, scale: jax.random.normal(k, shape, f32) * scale
    return {
        'x': nrm(ks[0], (BATCH, SEQ, D), 1.0),
        'a_w_qkv': nrm(ks[1], (N_A_LAYERS, D, A_QKV_DIM), D ** -0.5),
        'a_sinks': nrm(ks[2], (N_A_LAYERS, A_HEADS), 0.5),
        'a_w_o': nrm(ks[3], (N_A_LAYERS, A_HEADS * A_HEAD_DIM, D), BETA * (A_HEADS * A_HEAD_DIM) ** -0.5),
        'b_w_qkv': nrm(ks[4], (N_B_LAYERS, D, B_QKV_DIM), D ** -0.5),
        'b_lambda_q1': nrm(ks[5], (N_B_LAYERS, B_HEAD_DIM), 0.1),
        'b_lambda_k1': nrm(ks[6], (N_B_LAYERS, B_HEAD_DIM), 0.1),
        'b_lambda_q2': nrm(ks[7], (N_B_LAYERS, B_HEAD_DIM), 0.1),
        'b_lambda_k2': nrm(ks[8], (N_B_LAYERS, B_HEAD_DIM), 0.1),
        'b_subln_g': 1.0 + nrm(ks[9], (N_B_LAYERS, B_V_DIM), 0.02),
        'b_w_o': nrm(ks[10], (N_B_LAYERS, B_HEADS * B_V_DIM, D), BETA * (B_HEADS * B_V_DIM) ** -0.5),
        'ln1_g': 1.0 + nrm(ks[11], (DEPTH, D), 0.02),
        'ln1_b': nrm(ks[12], (DEPTH, D), 0.02),
        'ln2_g': 1.0 + nrm(ks[13], (DEPTH, D), 0.02),
        'ln2_b': nrm(ks[14], (DEPTH, D), 0.02),
        'peer_w_q': nrm(ks[15], (DEPTH, D, P_HEADS * P_KEY_DIM), D ** -0.5),
        'peer_subkeys': nrm(ks[16], (DEPTH, P_HEADS, 2, N_KEYS, P_HALF), P_HALF ** -0.5),
        'peer_u': nrm(ks[17], (DEPTH, N_EXPERTS, D), D ** -0.5),
        'peer_v': nrm(ks[18], (DEPTH, N_EXPERTS, D), BETA * P_HEADS ** -0.5),
    }

def reference(x, a_w_qkv, a_sinks, a_w_o, b_w_qkv, b_lambda_q1, b_lambda_k1, b_lambda_q2,
              b_lambda_k2, b_subln_g, b_w_o, ln1_g, ln1_b, ln2_g, ln2_b,
              peer_w_q, peer_subkeys, peer_u, peer_v):
    for i in range(DEPTH):
        j = i // N_MIXERS
        if i % N_MIXERS == 0:
            mix = sliding_window_gqa(x, a_w_qkv[j], a_sinks[j], a_w_o[j])
        else:
            lambda_init = 0.8 - 0.6 * math.exp(-0.3 * i)
            mix = differential_attention(x, b_w_qkv[j], b_lambda_q1[j], b_lambda_k1[j],
                                         b_lambda_q2[j], b_lambda_k2[j], b_subln_g[j],
                                         b_w_o[j], lambda_init)
        x = layer_norm(ALPHA * x + mix, ln1_g[i], ln1_b[i])
        ffn = peer_ffn(x, peer_w_q[i], peer_subkeys[i], peer_u[i], peer_v[i])
        x = layer_norm(ALPHA * x + ffn, ln2_g[i], ln2_b[i])
    return x


_drawn_inputs = setup_inputs


def setup_inputs(seed=0):
    import zlib

    import numpy as np

    out = dict(_drawn_inputs(seed))
    spreads = {}
    factors = {'a_sinks': 3.848,
     'b_lambda_q1': 8.0,
     'b_lambda_q2': 3.446,
     'b_lambda_k2': 4.894,
     'b_subln_g': 7.927}
    for name, (base, spread) in spreads.items():
        noise = np.random.default_rng([zlib.crc32(name.encode()), seed]).standard_normal(out[name].shape)
        drawn = base * np.exp(spread * noise) if base else spread * noise
        out[name] = __import__('jax').numpy.asarray(drawn.astype(out[name].dtype))
    for name, factor in factors.items():
        out[name] = (out[name] * factor).astype(out[name].dtype)
    return out
```

```python
import math
from contextlib import ExitStack

import numpy as np

import concourse.bass as bass
from concourse import mybir

ALU = mybir.AluOpType
ACT = mybir.ActivationFunctionType
F32 = mybir.dt.float32
U32 = mybir.dt.uint32
AX_X = mybir.AxisListType.X

P = 128
LN_EPS = 1e-5
MASKED = -1e32
LOWEST = -3.0e38
RING = 8


def alibi(n):
    return [float(s) for s in (2.0 ** (-8.0 * np.arange(1, n + 1) / n)).astype(np.float32)]


def decoder_trunk(nc, x, a_w_qkv, a_sinks, a_w_o, b_w_qkv, b_lambda_q1, b_lambda_k1, b_lambda_q2, b_lambda_k2,
                  b_subln_g, b_w_o, ln1_g, ln1_b, ln2_g, ln2_b, peer_w_q, peer_subkeys, peer_u, peer_v, out):
    _, SEQ, D = x.shape
    DEPTH = ln1_g.shape[0]
    A_HEADS = a_sinks.shape[1]
    HD = b_lambda_q1.shape[1]
    A_KV = (a_w_qkv.shape[2] // HD - A_HEADS) // 2
    VD = b_subln_g.shape[1]
    B_HEADS = b_w_o.shape[1] // VD
    PH, NKEYS, PHALF = peer_subkeys.shape[1], peer_subkeys.shape[3], peer_subkeys.shape[4]
    HC = 2 * PH
    TOPK = 16
    PICKS = PH * TOPK
    T = SEQ // P
    KT = D // P
    ALPHA = (2.0 * DEPTH) ** 0.25
    SCALE = HD ** -0.5
    GROUP = 512
    KK = 4
    CH = KT // KK
    BPG = GROUP // P
    assert T == 2 and D == 2048 and HD == 64 and PICKS == P and NKEYS == P and PHALF == P and DEPTH == 2
    slopes = [alibi(A_HEADS), alibi(B_HEADS)]

    QKV_GROUPS = [a_w_qkv.shape[2] // GROUP, b_w_qkv.shape[2] // GROUP]
    WO_GROUPS = D // GROUP
    WQ_GROUPS = D // GROUP
    LAYER_GROUPS = [n + WO_GROUPS + WQ_GROUPS for n in QKV_GROUPS]
    G0 = [0, LAYER_GROUPS[0]]
    JOBS = 2 * T * PICKS
    STEPS = 16
    NSUB = STEPS // T

    def wo_base(l):
        return G0[l] + QKV_GROUPS[l]

    def wq_base(l):
        return wo_base(l) + WO_GROUPS

    def group_done(g):
        return RING + (g + 1) * CH

    with ExitStack() as ctx:
        def sb(name, shape, dt=F32):
            return ctx.enter_context(nc.sbuf_tensor(name, shape, dt))

        def sem(name):
            return ctx.enter_context(nc.semaphore(name))

        ring = sb("ring", [P, RING, D])
        ring_w = ring[:, :, :].rearrange("p s (k n) -> p s k n", k=KK)
        xt = sb("xt", [P, T, D])
        xT = sb("xT", [P, KT, T * P])
        qT = sb("qT", [P, KT, T * P])
        kT = sb("kT", [P, KT, T * P])
        vn = sb("vn", [P, T, D])
        oT = sb("oT", [P, KT, T * P])
        gb = sb("gb", [P, 2, D])
        skT = oT[:, 0:HC // 2, :].rearrange("p a (b k) -> p (a b) k", k=NKEYS)
        wide = sb("wide", [P, 2, 1024])
        pT = sb("pT", [P, 2, 1024])
        ident = sb("ident", [P, P])
        mask = sb("mask", [P, 2, 2 * P])
        iota16 = sb("iota16", [P, TOPK])
        sink8 = sb("sink8", [P, A_HEADS])
        lamv = sb("lamv", [P, 4, HD])
        subg = sb("subg", [P, VD])
        sm = sb("sm", [P, 64])
        mx = sb("mx", [P, 2, 4])
        nm = sb("nm", [P, 2, 4])
        rs = sb("rs", [P, 2, 4])
        sk = sb("sk", [P, 2, 4])
        rd = sb("rd", [P, 2, 4])
        stats = sb("stats", [P, 4, 6])
        mv = sb("mv", [P, 4])
        top = sb("top", [P, HC, TOPK])
        topi = sb("topi", [P, HC, TOPK], U32)
        topf = sb("topf", [P, HC, TOPK])
        best = sb("best", [P, PH, TOPK])
        pos = sb("pos", [P, 3, PH * TOPK], U32)
        posf = sb("posf", [P, 2, PH * TOPK])
        key = sb("key", [P, 2, PH * TOPK])
        gsum = sb("gsum", [P, 2, PH])
        idx = sb("idx", [P, T, PICKS], U32)
        idxs = sb("idxs", [P, 2, RING], U32)
        gate = sb("gate", [P, T, PICKS])
        act8 = sb("act8", [P, RING])
        act = sb("act", [P, T, PICKS])
        ps = ctx.enter_context(nc.psum_tensor("ps", [P, 8, 512], F32))

        x_in = [sem(f"x_in{t}") for t in range(T)]
        small_in = sem("small_in")
        gb_in = sem("gb_in")
        sk_in = sem("sk_in")
        w_in = [sem(f"w_in{r}") for r in range(RING)]
        w_free = sem("w_free")
        rows_in = [sem(f"rows_in{r}") for r in range(RING)]
        slot_free = sem("slot_free")
        idx_staged = sem("idx_staged")
        gathers_begun = sem("gathers_begun")
        out_done = sem("out_done")
        const_pool = sem("const_pool")
        xT_done = sem("xT_done")
        xT_moved = sem("xT_moved")
        proj_free = sem("proj_free")
        sc_done = sem("sc_done")
        sc_ready = sem("sc_ready")
        sc_exp = sem("sc_exp")
        prob_ready = sem("prob_ready")
        pt_done = sem("pt_done")
        pt_moved = sem("pt_moved")
        pv_done = sem("pv_done")
        pv_moved = sem("pv_moved")
        sub_sq = sem("sub_sq")
        sub_rt = sem("sub_rt")
        sub_done = sem("sub_done")
        ot_done = sem("ot_done")
        ot_moved = sem("ot_moved")
        lam_dot = sem("lam_dot")
        lam_exp = sem("lam_exp")
        ln_var = sem("ln_var")
        ln_root = sem("ln_root")
        ln_done = sem("ln_done")
        skT_done = sem("skT_done")
        skT_moved = sem("skT_moved")
        rt_done = sem("rt_done")
        rt_moved = sem("rt_moved")
        gate_sub = sem("gate_sub")
        gate_exp = sem("gate_exp")
        routed = sem("routed")
        gelu_done = sem("gelu_done")
        dots_kept = sem("dots_kept")
        dve_step = sem("dve_step")
        act_step = sem("act_step")

        w_qkv = [a_w_qkv[0], b_w_qkv[0]]
        w_o = [a_w_o[0], b_w_o[0]]

        def chunks_of(w):
            return w.rearrange("(q k p) n -> q p k n", p=P, k=KK)

        block = ctx.enter_context(nc.Block())

        @block.sync
        def _(sp):
            for t in range(T):
                sp.dma_start(xt[:, t, :], x[0, t * P:(t + 1) * P, :]).then_inc(x_in[t], 16)

            def stream(w, base, groups, col0=0):
                wc = chunks_of(w)
                pairs = groups // 2

                def pair(it, cols, n):
                    for i in range(n * CH):
                        c = base * CH + i
                        sp.wait_ge(w_free, it * (2 * CH) + c + 1)
                        src = wc[i % CH][:, :, bass.ds(cols + (i // CH) * GROUP, GROUP)]
                        sp.dma_start(ring_w[:, c % RING], src).then_inc(w_in[c % RING], 16)

                if pairs:
                    with sp.Fori(0, pairs) as it:
                        pair(it, it * (2 * GROUP) + col0, 2)
                if groups % 2:
                    base += 2 * pairs
                    pair(0, col0 + 2 * pairs * GROUP, 1)

            for l in range(DEPTH):
                if l:
                    sp.wait_ge(slot_free, RING + l * JOBS)
                stream(w_qkv[l], G0[l], QKV_GROUPS[l])
                if l:
                    sp.wait_ge(ln_done, 2 * T * l)
                for j, v in enumerate((ln1_g, ln1_b)):
                    sp.dma_start(gb[:, j, :], v[l:l + 1, :].broadcast_to([P, D])).then_inc(gb_in, 16)
                stream(w_o[l], wo_base(l), WO_GROUPS)
                sp.wait_ge(pv_moved, STEPS * (l + 1))
                sp.dma_start(kT[:, 0:KT // 2, :].rearrange("p k n -> p (k n)").rearrange("p (c d) -> p c d", d=PHALF),
                             peer_subkeys[l].rearrange("h c k d -> k (h c) d")).then_inc(sk_in, 16)
                stream(peer_w_q[l], wq_base(l), WQ_GROUPS)
                sp.wait_ge(ln_done, 2 * T * l + T)
                for j, v in enumerate((ln2_g, ln2_b)):
                    sp.dma_start(gb[:, j, :], v[l:l + 1, :].broadcast_to([P, D])).then_inc(gb_in, 16)
            for t in range(T):
                sp.wait_ge(ln_done, 2 * T * (DEPTH - 1) + T + t + 1)
                sp.dma_start(out[0, t * P:(t + 1) * P, :], xt[:, t, :]).then_inc(out_done, 16)
            sp.wait_ge(out_done, 16 * T)

        @block.gpsimd
        def _(pool):
            pool.memset(ident[:], 0.0).then_inc(const_pool, 1)
            for m in range(2):
                pool.iota(mask[:, m, :], [[1, 2 * P]], base=-P, channel_multiplier=-1,
                          allow_small_or_imprecise_dtypes=True).then_inc(const_pool, 1)
            pool.iota(iota16[:], [[1, TOPK]], base=0, channel_multiplier=0,
                      allow_small_or_imprecise_dtypes=True).then_inc(const_pool, 1)
            pool.wait_ge(const_pool, 4)
            pool.affine_select(out=ident[:], in_=ident[:], compare_op=ALU.not_equal, fill=1.0, base=0,
                               pattern=[[-1, P]], channel_multiplier=1).then_inc(const_pool, 1)
            for m in range(2):
                pool.affine_select(out=mask[:, m, :], in_=mask[:, m, :], compare_op=ALU.is_ge, fill=MASKED, base=P,
                                   pattern=[[-1, 2 * P]], channel_multiplier=1).then_inc(const_pool, 1)
            pool.wait_ge(const_pool, 7)
            pool.affine_select(out=mask[:, 0, :], in_=mask[:, 0, :], compare_op=ALU.is_ge, fill=MASKED, base=-1,
                               pattern=[[1, 2 * P]], channel_multiplier=-1).then_inc(const_pool, 1)

            for l in range(DEPTH):
                for s in range(2 * T):
                    t, table = s % T, (peer_u if s < T else peer_v)
                    rows = table.rearrange("l e d -> (l e) d")
                    job0 = l * JOBS + s * PICKS
                    pool.wait_ge(routed, l * T + t + 1)
                    with pool.Fori(0, PICKS // (2 * RING)) as it:
                        for half in range(2):
                            pool.tensor_copy(idxs[:, half, :], idx[:, t, bass.ds(it * (2 * RING) + half * RING, RING)]
                                             ).then_inc(idx_staged, 1)
                            pool.wait_ge(idx_staged, it * 2 + job0 // RING + half + 1)
                            for r in range(RING):
                                pool.wait_ge(slot_free, it * (2 * RING) + job0 + half * RING + r + 1)
                                pool.sem_inc(gathers_begun, 1)
                                pool.indirect_dma_start(
                                    out=ring[:, r, :], out_offset=None, in_=rows,
                                    in_offset=bass.IndirectOffsetOnAxis(ap=idxs[:, half, r:r + 1], axis=0),
                                ).then_inc(rows_in[r], 16)

        @block.scalar
        def _(a):
            a.sem_inc(proj_free, 2)
            a.dma_start(sink8[:], a_sinks[0:1, :].broadcast_to([P, A_HEADS])).then_inc(small_in, 16)
            for j, v in enumerate((b_lambda_q1, b_lambda_k1, b_lambda_q2, b_lambda_k2)):
                a.dma_start(lamv[:, j, :], v[0:1, :].broadcast_to([P, HD])).then_inc(small_in, 16)
            a.dma_start(subg[:], b_subln_g[0:1, :].broadcast_to([P, VD])).then_inc(small_in, 16)

            def move_xT(n):
                for t in range(T):
                    for b in range(4):
                        a.wait_ge(xT_done, (n * T + t) * 4 + b + 1)
                        a.copy(xT[:, 4 * b:4 * b + 4, t * P:(t + 1) * P],
                               ps[:, 4 + b, :].rearrange("p (k n) -> p k n", n=P)).then_inc(xT_moved, 1)

            def move_transposed(dst, base, groups):
                with a.Fori(0, groups // 2) as it:
                    for i in range(2):
                        g = base + i
                        a.wait_ge(w_free, it * 2 * CH + group_done(g))
                        for b in range(2):
                            last = a.copy(dst[:, bass.ds(it * (2 * BPG) + i * BPG + 2 * b, 2), :],
                                          ps[:, 2 * (g % 2) + b, :].rearrange("p (k n) -> p k n", n=T * P))
                        last.then_inc(proj_free, 1)

            def move_rows(dst, base, groups):
                with a.Fori(0, groups // 2) as it:
                    for i in range(2):
                        g = base + i
                        a.wait_ge(w_free, it * 2 * CH + group_done(g))
                        for t in range(T):
                            last = a.copy(dst[:, t, bass.ds(it * (2 * GROUP) + i * GROUP, GROUP)],
                                          ps[:, 2 * (g % 2) + t, :])
                        last.then_inc(proj_free, 1)

            def root(n):
                a.wait_ge(ln_var, n + 1)
                a.activation(mv[:, 2:3], mv[:, 1:2], ACT.Sqrt).then_inc(ln_root, 1)

            def attention(l):
                for i in range(STEPS + 1):
                    if i < STEPS:
                        n = l * STEPS + i
                        t = i // NSUB
                        w = P * (t + 1)
                        a.wait_ge(sc_ready, n + 1)
                        s4 = wide[:, i % 2, :].rearrange("p (m k) -> p m k", k=2 * P)
                        for m in range(4):
                            last = a.activation(s4[:, m, 0:w], s4[:, m, 0:w], ACT.Exp, bias=nm[:, i % 2, m:m + 1],
                                                scale=SCALE, accum_out=rs[:, i % 2, m:m + 1])
                        if l == 0:
                            last = a.activation(sk[:, i % 2, :], sk[:, i % 2, :], ACT.Exp)
                        last.then_inc(sc_exp, 1)
                    if i:
                        j = i - 1
                        n = l * STEPS + j
                        nb = j // NSUB + 1
                        cols = 4 * P if l == 0 else 2 * P
                        a.wait_ge(pt_done, n + 1)
                        if j >= 2:
                            a.wait_ge(pv_done, n - 1)
                        for b in range(nb):
                            last = a.copy(pT[:, j % 2, b * 512:b * 512 + cols], ps[:, 4 + b, 0:cols])
                        last.then_inc(pt_moved, 1)

            for l in range(DEPTH):
                if l == 0:
                    move_xT(0)
                    move_transposed(qT, 0, 4)
                    a.wait_ge(w_free, group_done(4))
                    a.copy(kT[:, 0:2, :], ps[:, 0, :].rearrange("p (k n) -> p k n", n=T * P))
                    a.copy(kT[:, 2:4, :], ps[:, 1, :].rearrange("p (k n) -> p k n", n=T * P))
                    a.copy(vn[:, :, 0:A_KV * HD], ps[:, 4, :].rearrange("p (t n) -> p t n", t=T)).then_inc(proj_free, 1)
                else:
                    a.wait_ge(lam_dot, 2)
                    a.activation(sm[:, 2:4], sm[:, 0:2], ACT.Exp).then_inc(lam_exp, 1)
                    move_xT(2)
                    move_transposed(qT, G0[l], 4)
                    move_transposed(kT, G0[l] + 4, 4)
                    move_rows(vn, G0[l] + 8, 4)
                attention(l)
                if l == 1:
                    for t in range(T):
                        a.wait_ge(sub_sq, t + 1)
                        a.activation(sm[:, 24:40], sm[:, 8:24], ACT.Sqrt).then_inc(sub_rt, 1)
                    for t in range(T):
                        for b in range(4):
                            a.wait_ge(ot_done, t * 4 + b + 1)
                            a.copy(oT[:, 4 * b:4 * b + 4, t * P:(t + 1) * P],
                                   ps[:, 4 + b, :].rearrange("p (k n) -> p k n", n=P)).then_inc(ot_moved, 1)
                for b in range(4):
                    a.wait_ge(skT_done, l * 4 + b + 1)
                    a.copy(skT[:, 4 * b:4 * b + 4, :], ps[:, 4 + b, :].rearrange("p (k n) -> p k n", n=P)
                           ).then_inc(skT_moved, 1)
                for t in range(T):
                    root(2 * T * l + t)
                move_xT(2 * l + 1)
                move_transposed(qT, wq_base(l), 4)
                for t in range(T):
                    a.wait_ge(rt_done, T * l + t + 1)
                    dst = wide if t == 0 else pT
                    for b in range(4):
                        last = a.copy(dst[:, b // 2, (b % 2) * 512:(b % 2) * 512 + 512], ps[:, 4 * (1 - t) + b, :])
                    last.then_inc(rt_moved, 1)
                for t in range(T):
                    a.wait_ge(gate_sub, T * l + t + 1)
                    a.activation(gate[:, t, :], gate[:, t, :], ACT.Exp).then_inc(gate_exp, 1)
                for t in range(T):
                    a.wait_ge(dots_kept, (T * l + t + 1) * (PICKS // RING) + 1)
                    a.activation(act[:, t, :], act[:, t, :], ACT.Gelu).then_inc(gelu_done, 1)
                for t in range(T):
                    root(2 * T * l + T + t)

        @block.tensor
        def _(pe):
            def transpose_x(n):
                for t in range(T):
                    if n == 0:
                        pe.wait_ge(x_in[t], 16)
                        pe.wait_ge(const_pool, 5)
                    else:
                        pe.wait_ge(ln_done, T * (n - 1) + t + 1)
                    for k in range(KT):
                        b = k // 4
                        if k % 4 == 0 and n * T + t > 0:
                            pe.wait_ge(xT_moved, (n * T + t - 1) * 4 + b + 1)
                        last = pe.transpose(ps[:, 4 + b, (k % 4) * P:(k % 4 + 1) * P], xt[:, t, k * P:(k + 1) * P],
                                            ident[:])
                        if k % 4 == 3:
                            last.then_inc(xT_done, 1)

            def project(base, groups, src, by_rows, done_first=None):
                with pe.Fori(0, groups // 2) as it:
                    for i in range(2):
                        g = base + i
                        pe.wait_ge(proj_free, it * 2 + g + 1)
                        for q in range(CH):
                            c = g * CH + q
                            pe.wait_ge(w_in[c % RING], it * 16 + 16 * (c // RING + 1))
                            for kk in range(KK):
                                k = q * KK + kk
                                w = ring_w[:, c % RING, kk, :]
                                if by_rows:
                                    for t in range(T):
                                        last = pe.matmul(ps[:, 2 * (g % 2) + t, :], src[:, k, t * P:(t + 1) * P], w,
                                                         start=(k == 0), stop=(k == KT - 1))
                                else:
                                    for b in range(BPG):
                                        last = pe.matmul(
                                            ps[:, 2 * (g % 2) + b // 2, (b % 2) * 256:(b % 2) * 256 + 256],
                                            w[:, b * P:(b + 1) * P], src[:, k, :], start=(k == 0 and b % 2 == 0),
                                            stop=(k == KT - 1), skip_group_check=True)
                            last.then_inc(w_free, 1)

            def attention(l):
                def scores(i):
                    n, t, hg = l * STEPS + i, i // NSUB, i % NSUB
                    w = P * (t + 1)
                    if i >= 2:
                        pe.wait_ge(sc_ready, n - 1)
                    for m in range(4):
                        at = slice(HD * (m % 2), HD * (m % 2) + HD)
                        keys = kT[at, hg // 2, 0:w] if l == 0 else kT[at, 2 * hg + m // 2, 0:w]
                        last = pe.matmul(ps[:, 2 * (i % 2) + m % 2, (m // 2) * 256:(m // 2) * 256 + w],
                                         qT[at, 2 * hg + m // 2, t * P:(t + 1) * P], keys, start=True, stop=True)
                    last.then_inc(sc_done, 1)

                def turn(i):
                    n, t = l * STEPS + i, i // NSUB
                    pe.wait_ge(prob_ready, n + 1)
                    if i:
                        pe.wait_ge(pt_moved, n)
                    s4 = wide[:, i % 2, :].rearrange("p (m k) -> p m k", k=2 * P)
                    for b in range(t + 1):
                        for j, m in enumerate((0, 2, 1, 3) if l == 0 else (0, 2)):
                            last = pe.transpose(ps[:, 4 + b, j * P:(j + 1) * P], s4[:, m, b * P:(b + 1) * P], ident[:])
                    last.then_inc(pt_done, 1)

                def values(i):
                    n, t, hg = l * STEPS + i, i // NSUB, i % NSUB
                    pe.wait_ge(pt_moved, n + 1)
                    if i >= 2:
                        pe.wait_ge(pv_moved, n - 1)
                    for j in range(2):
                        for b in range(t + 1):
                            flags = dict(start=(b == 0), stop=(b == t))
                            if l == 0:
                                last = pe.matmul(ps[HD * j:HD * j + HD, 6 + i % 2, 0:2 * P],
                                                 vn[:, b, (hg // 2) * HD:(hg // 2 + 1) * HD],
                                                 pT[:, i % 2, b * 512 + 2 * j * P:b * 512 + 2 * (j + 1) * P], **flags)
                            else:
                                h = 2 * hg + j
                                last = pe.matmul(ps[:, 6 + i % 2, j * VD:(j + 1) * VD],
                                                 pT[:, i % 2, b * 512 + j * P:b * 512 + (j + 1) * P],
                                                 vn[:, b, h * VD:(h + 1) * VD], **flags)
                    last.then_inc(pv_done, 1)

                for i in range(STEPS + 2):
                    if i < STEPS:
                        scores(i)
                    if 1 <= i <= STEPS:
                        turn(i - 1)
                    if i >= 2:
                        values(i - 2)

            for l in range(DEPTH):
                transpose_x(2 * l)
                pe.wait_ge(xT_moved, (2 * l + 1) * 4 * T)
                if l == 0:
                    project(0, 4, xT, False)
                    g = 4
                    pe.wait_ge(proj_free, g + 1)
                    for q in range(CH):
                        c = g * CH + q
                        pe.wait_ge(w_in[c % RING], 16 * (c // RING + 1))
                        for kk in range(KK):
                            k = q * KK + kk
                            w = ring_w[:, c % RING, kk, :]
                            flags = dict(stop=(k == KT - 1), skip_group_check=True)
                            for h in range(A_KV):
                                for half in range(2):
                                    pe.matmul(ps[HD * half:HD * half + HD, h // 2, (h % 2) * 256:(h % 2) * 256 + 256],
                                              w[:, h * HD:(h + 1) * HD], xT[:, k, :],
                                              start=(k == 0 and h % 2 == 0), **flags)
                            for t in range(T):
                                last = pe.matmul(ps[:, 4, t * 256:(t + 1) * 256], xT[:, k, t * P:(t + 1) * P],
                                                 w[:, A_KV * HD:2 * A_KV * HD], start=(k == 0 and t == 0), **flags)
                        last.then_inc(w_free, 1)
                else:
                    project(G0[l], 8, xT, False)
                    project(G0[l] + 8, 4, xT, True)
                pe.wait_ge(proj_free, wo_base(l) + 2)
                attention(l)
                if l == 1:
                    for t in range(T):
                        pe.wait_ge(sub_done, t + 1)
                        for k in range(KT):
                            b = k // 4
                            if t and k % 4 == 0:
                                pe.wait_ge(ot_moved, b + 1)
                            last = pe.transpose(ps[:, 4 + b, (k % 4) * P:(k % 4 + 1) * P],
                                                xT[:, 8 * t + k // 2, (k % 2) * P:(k % 2 + 1) * P], ident[:])
                            if k % 4 == 3:
                                last.then_inc(ot_done, 1)
                    pe.wait_ge(ot_moved, 4 * T)
                else:
                    pe.wait_ge(pv_moved, STEPS)
                project(wo_base(l), 4, oT, True)
                pe.wait_ge(sk_in, 16 * (l + 1))
                for k in range(HC):
                    last = pe.transpose(ps[:, 4 + k // 4, (k % 4) * P:(k % 4 + 1) * P],
                                        kT[:, k // 2, (k % 2) * P:(k % 2 + 1) * P], ident[:])
                    if k % 4 == 3:
                        last.then_inc(skT_done, 1)
                pe.wait_ge(skT_moved, 4 * (l + 1))
                transpose_x(2 * l + 1)
                pe.wait_ge(xT_moved, (2 * l + 2) * 4 * T)
                project(wq_base(l), 4, xT, False)
                pe.wait_ge(proj_free, G0[l] + LAYER_GROUPS[l] + 2)
                for t in range(T):
                    for j in range(HC):
                        last = pe.matmul(ps[:, 4 * (1 - t) + j // 4, (j % 4) * P:(j % 4 + 1) * P],
                                         qT[:, j, t * P:(t + 1) * P], skT[:, j, :], start=True, stop=True)
                    last.then_inc(rt_done, 1)

        @block.vector
        def _(v):
            own = [0]

            def step(ins):
                ins.then_inc(dve_step, 1)
                own[0] += 1
                v.wait_ge(dve_step, own[0])

            v.sem_inc(w_free, RING)
            v.sem_inc(slot_free, RING)

            def layer_norm(n, t, l):
                for c in range(4):
                    last = v.bn_stats(stats[:, c, :], xt[:, t, c * 512:(c + 1) * 512])
                step(last)
                step(v.bn_aggr(mv[:, 0:2], stats[:].rearrange("p a b -> p (a b)")))
                v.tensor_scalar(mv[:, 1:2], mv[:, 1:2], LN_EPS, None, ALU.add).then_inc(ln_var, 1)
                v.wait_ge(ln_root, n + 1)
                step(v.reciprocal(mv[:, 3:4], mv[:, 2:3]))
                step(v.tensor_scalar(xt[:, t, :], xt[:, t, :], mv[:, 0:1], mv[:, 3:4], ALU.subtract, ALU.mult))
                v.wait_ge(gb_in, 32 * (n // T + 1))
                step(v.tensor_tensor(xt[:, t, :], xt[:, t, :], gb[:, 0, :], ALU.mult))
                v.tensor_tensor(xt[:, t, :], xt[:, t, :], gb[:, 1, :], ALU.add).then_inc(ln_done, 1)

            def attention(l):
                def bias(i):
                    n, t, hg = l * STEPS + i, i // NSUB, i % NSUB
                    w = P * (t + 1)
                    v.wait_ge(sc_done, n + 1)
                    if i >= 2:
                        v.wait_ge(pt_done, n - 1)
                    s4 = wide[:, i % 2, :].rearrange("p (m k) -> p m k", k=2 * P)
                    for m in range(4):
                        slope = slopes[0][4 * hg + m] if l == 0 else slopes[1][2 * hg + m // 2]
                        last = v.scalar_tensor_tensor(
                            out=s4[:, m, 0:w], in0=mask[:, l, 2 * P - w:2 * P], scalar=slope / SCALE,
                            in1=ps[:, 2 * (i % 2) + m % 2, (m // 2) * 256:(m // 2) * 256 + w],
                            op0=ALU.mult, op1=ALU.add)
                    step(last)
                    step(v.tensor_reduce(mx[:, i % 2, :], s4[:, :, 0:w], AX_X, ALU.max))
                    if l == 0:
                        step(v.tensor_tensor(mx[:, i % 2, :], mx[:, i % 2, :], sink8[:, 4 * hg:4 * hg + 4], ALU.max))
                        v.tensor_tensor(sk[:, i % 2, :], sink8[:, 4 * hg:4 * hg + 4], mx[:, i % 2, :], ALU.subtract)
                        step(v.tensor_scalar(nm[:, i % 2, :], mx[:, i % 2, :], -SCALE, None, ALU.mult))
                        v.tensor_scalar(sk[:, i % 2, :], sk[:, i % 2, :], SCALE, None, ALU.mult).then_inc(sc_ready, 1)
                    else:
                        v.tensor_scalar(nm[:, i % 2, :], mx[:, i % 2, :], -SCALE, None, ALU.mult).then_inc(sc_ready, 1)

                def norm(i):
                    n, t = l * STEPS + i, i // NSUB
                    w = P * (t + 1)
                    v.wait_ge(sc_exp, n + 1)
                    s4 = wide[:, i % 2, :].rearrange("p (m k) -> p m k", k=2 * P)
                    if l == 0:
                        step(v.tensor_tensor(rd[:, i % 2, :], rs[:, i % 2, :], sk[:, i % 2, :], ALU.add))
                        step(v.reciprocal(rd[:, i % 2, :], rd[:, i % 2, :]))
                        for m in range(4):
                            last = v.tensor_scalar(s4[:, m, 0:w], s4[:, m, 0:w], rd[:, i % 2, m:m + 1], None, ALU.mult)
                    else:
                        step(v.reciprocal(rd[:, i % 2, :], rs[:, i % 2, :]))
                        step(v.tensor_scalar(rd[:, i % 2, 1:4:2], rd[:, i % 2, 1:4:2], sm[:, 5:6], None, ALU.mult))
                        for m in (1, 3):
                            last = v.tensor_scalar(s4[:, m, 0:w], s4[:, m, 0:w], rd[:, i % 2, m:m + 1], None, ALU.mult)
                        step(last)
                        for m in (0, 2):
                            last = v.scalar_tensor_tensor(out=s4[:, m, 0:w], in0=s4[:, m, 0:w],
                                                          scalar=rd[:, i % 2, m:m + 1], in1=s4[:, m + 1, 0:w],
                                                          op0=ALU.mult, op1=ALU.add)
                    last.then_inc(prob_ready, 1)

                def move(i):
                    n, t, hg = l * STEPS + i, i // NSUB, i % NSUB
                    v.wait_ge(pv_done, n + 1)
                    if l == 0:
                        dst = oT[:, 2 * hg:2 * hg + 2, t * P:(t + 1) * P]
                        src = ps[:, 6 + i % 2, 0:2 * P].rearrange("p (j q) -> p j q", q=P)
                    else:
                        dst = xT[:, 8 * t + hg, :]
                        src = ps[:, 6 + i % 2, 0:2 * VD]
                    v.tensor_copy(dst, src).then_inc(pv_moved, 1)

                for i in range(STEPS + 3):
                    if i < STEPS:
                        bias(i)
                    if 1 <= i <= STEPS:
                        norm(i - 1)
                    if i >= 3:
                        move(i - 3)

            def sub_norm(l):
                li = 0.8 - 0.6 * math.exp(-0.3 * l)
                for t in range(T):
                    o = xT[:, 8 * t:8 * t + 8, :].rearrange("p a b -> p (a b)")
                    o3 = o.rearrange("p (h e) -> p h e", e=VD)
                    w3 = wide[:].rearrange("p a (h e) -> p (a h) e", e=VD)
                    if t == 0:
                        v.wait_ge(pv_moved, STEPS * (l + 1))
                        v.wait_ge(pt_done, STEPS * (l + 1))
                    step(v.tensor_tensor(wide[:].rearrange("p a b -> p (a b)"), o, o, ALU.mult))
                    step(v.tensor_reduce(sm[:, 8:24], w3, AX_X, ALU.add))
                    v.tensor_scalar(sm[:, 8:24], sm[:, 8:24], 1.0 / VD, LN_EPS, ALU.mult, ALU.add).then_inc(sub_sq, 1)
                    v.wait_ge(sub_rt, t + 1)
                    step(v.reciprocal(sm[:, 40:56], sm[:, 24:40]))
                    step(v.tensor_scalar(sm[:, 40:56], sm[:, 40:56], 1.0 - li, None, ALU.mult))
                    step(v.tensor_tensor(o3, o3, sm[:, 40:56].unsqueeze(2).broadcast_to([P, B_HEADS, VD]), ALU.mult))
                    v.tensor_tensor(o3, o3, subg[:].unsqueeze(1).broadcast_to([P, B_HEADS, VD]), ALU.mult
                                    ).then_inc(sub_done, 1)

            def route(l, t):
                sc = (wide if t == 0 else pT)[:].rearrange("p a (j k) -> p (a j) k", k=NKEYS)
                v.wait_ge(rt_moved, T * l + t + 1)

                def top16(n, values, out_v, out_i):
                    for half in range(2):
                        at = slice(8 * half, 8 * half + 8)
                        for j in range(n):
                            last = v.max(out_v(j)[:, at], values(j))
                        step(last)
                        for j in range(n):
                            last = v.max_index(out_i(j)[:, at], out_v(j)[:, at], values(j))
                        step(last)
                        if half == 0:
                            for j in range(n):
                                last = v.match_replace(values(j), out_v(j)[:, at], values(j), LOWEST)
                            step(last)

                top16(HC, lambda j: sc[:, j, :], lambda j: top[:, j, :], lambda j: topi[:, j, :])
                v.tensor_copy(topf[:], topi[:])
                cand = vn[:, t, :].rearrange("p (h i j) -> p h i j", i=TOPK, j=TOPK)
                halves = top[:].rearrange("p (h c) k -> p h c k", c=2)
                step(v.tensor_tensor(cand, halves[:, :, 0, :].unsqueeze(3).broadcast_to([P, PH, TOPK, TOPK]),
                                     halves[:, :, 1, :].unsqueeze(2).broadcast_to([P, PH, TOPK, TOPK]), ALU.add))
                cand_h = vn[:, t, :].rearrange("p (h n) -> p h n", h=PH)
                pos_h = pos[:, 0, :].rearrange("p (h k) -> p h k", h=PH)
                top16(PH, lambda h: cand_h[:, h, :], lambda h: best[:, h, :], lambda h: pos_h[:, h, :])
                gate_h = gate[:, t, :].rearrange("p (h k) -> p h k", h=PH)
                v.tensor_tensor(gate_h, best[:], best[:, :, 0:1].broadcast_to([P, PH, TOPK]), ALU.subtract
                                ).then_inc(gate_sub, 1)
                v.tensor_scalar(pos[:, 1, :], pos[:, 0, :], 4, None, ALU.logical_shift_right)
                step(v.tensor_scalar(pos[:, 2, :], pos[:, 0, :], TOPK - 1, None, ALU.bitwise_and))
                step(v.tensor_copy(posf[:], pos[:, 1:3, :]))
                keys = topf[:].rearrange("p (h c) k -> p h c k", c=2)
                hot = [kT[:, 8 * c:8 * c + 8, :].rearrange("p a (n k) -> p (a n) k", k=TOPK) for c in range(2)]
                for c in range(2):
                    last = v.tensor_tensor(hot[c], posf[:, c, :].unsqueeze(2).broadcast_to([P, PICKS, TOPK]),
                                           iota16[:].unsqueeze(1).broadcast_to([P, PICKS, TOPK]), ALU.is_equal)
                step(last)
                for c in range(2):
                    h4 = hot[c].rearrange("p (h n) k -> p h n k", h=PH)
                    last = v.tensor_tensor(h4, h4, keys[:, :, c, :].unsqueeze(2).broadcast_to([P, PH, TOPK, TOPK]),
                                           ALU.mult)
                step(last)
                for c in range(2):
                    last = v.tensor_reduce(key[:, c, :], hot[c], AX_X, ALU.add)
                step(last)
                if l:
                    step(v.tensor_scalar(key[:, 1, :], key[:, 1, :], float(l * NKEYS * NKEYS), None, ALU.add))
                v.scalar_tensor_tensor(out=idx[:, t, :], in0=key[:, 0, :], scalar=float(NKEYS), in1=key[:, 1, :],
                                       op0=ALU.mult, op1=ALU.add).then_inc(routed, 1)
                v.wait_ge(gate_exp, T * l + t + 1)
                step(v.tensor_reduce(gsum[:, 0, :], gate_h, AX_X, ALU.add))
                step(v.reciprocal(gsum[:, 1, :], gsum[:, 0, :]))
                step(v.tensor_tensor(gate_h, gate_h, gsum[:, 1, :].unsqueeze(2).broadcast_to([P, PH, TOPK]), ALU.mult))

            def dots(l, t):
                job0 = l * JOBS + t * PICKS
                seq0 = (l * T + t) * (PICKS // RING)
                with v.Fori(0, PICKS // RING) as it:
                    v.wait_ge(dots_kept, it + seq0 + 1)
                    for r in range(RING):
                        v.wait_ge(rows_in[r], it * 16 + 16 * (job0 // RING + 1))
                        v.tensor_tensor_reduce(ring[:, r, :], ring[:, r, :], xt[:, t, :], 1.0, 0.0, ALU.mult, ALU.add,
                                               act8[:, r:r + 1]).then_inc(slot_free, 1)
                    v.wait_ge(slot_free, it * RING + job0 + 2 * RING)
                    v.tensor_copy(act[:, t, bass.ds(it * RING, RING)], act8[:]).then_inc(dots_kept, 1)

            def weigh(l, t):
                v.wait_ge(gelu_done, T * l + t + 1)
                step(v.tensor_tensor(act[:, t, :], gate[:, t, :], act[:, t, :], ALU.mult))

            def accumulate(l, t):
                job0 = l * JOBS + (T + t) * PICKS
                acc = ps[:, 4 * (1 - t):4 * (1 - t) + 4, :].rearrange("p b n -> p (b n)")
                step(v.memset(acc, 0.0))
                with v.Fori(0, PICKS // RING) as it:
                    for r in range(RING):
                        v.wait_ge(rows_in[r], it * 16 + 16 * (job0 // RING + 1))
                        v.scalar_tensor_tensor(out=acc, in0=ring[:, r, :], scalar=act[:, t, bass.ds(it * RING + r, 1)],
                                               in1=acc, op0=ALU.mult, op1=ALU.add).then_inc(slot_free, 1)
                        v.wait_ge(slot_free, it * RING + job0 + RING + r + 1)
                step(v.scalar_tensor_tensor(out=xt[:, t, :], in0=xt[:, t, :], scalar=ALPHA, in1=acc,
                                            op0=ALU.mult, op1=ALU.add))

            v.sem_inc(dots_kept, 1)
            v.wait_ge(small_in, 6 * 16)
            step(v.tensor_scalar(sink8[:], sink8[:], 1.0 / SCALE, None, ALU.mult))
            for j in range(2):
                v.tensor_tensor_reduce(lamv[:, 2 * j, :], lamv[:, 2 * j, :], lamv[:, 2 * j + 1, :], 1.0, 0.0, ALU.mult,
                                       ALU.add, sm[:, j:j + 1]).then_inc(lam_dot, 1)
            v.wait_ge(const_pool, 8)
            for l in range(DEPTH):
                if l == 1:
                    v.wait_ge(lam_exp, 1)
                    step(v.tensor_tensor(sm[:, 4:5], sm[:, 3:4], sm[:, 2:3], ALU.subtract))
                    step(v.tensor_scalar(sm[:, 5:6], sm[:, 4:5], -(0.8 - 0.6 * math.exp(-0.3 * l)), None, ALU.add))
                attention(l)
                if l == 1:
                    sub_norm(l)
                base = wo_base(l)
                with v.Fori(0, WO_GROUPS // 2) as it:
                    for i in range(2):
                        g = base + i
                        v.wait_ge(w_free, it * 2 * CH + group_done(g))
                        for t in range(T):
                            xs = xt[:, t, bass.ds(it * (2 * GROUP) + i * GROUP, GROUP)]
                            last = v.scalar_tensor_tensor(out=xs, in0=xs, scalar=ALPHA, in1=ps[:, 2 * (g % 2) + t, :],
                                                          op0=ALU.mult, op1=ALU.add)
                        last.then_inc(proj_free, 1)
                v.wait_ge(proj_free, base + WO_GROUPS + 2)
                for t in range(T):
                    layer_norm(2 * T * l + t, t, l)
                for t in range(T):
                    route(l, t)
                for t in range(T):
                    dots(l, t)
                    if t:
                        weigh(l, t - 1)
                weigh(l, T - 1)
                for t in range(T):
                    accumulate(l, t)
                    layer_norm(2 * T * l + T + t, t, l)


_INS = ['x', 'a_w_qkv', 'a_sinks', 'a_w_o', 'b_w_qkv', 'b_lambda_q1', 'b_lambda_k1', 'b_lambda_q2', 'b_lambda_k2',
        'b_subln_g', 'b_w_o', 'ln1_g', 'ln1_b', 'ln2_g', 'ln2_b', 'peer_w_q', 'peer_subkeys', 'peer_u', 'peer_v']


def kernel(**inputs):
    import numpy as _np
    import concourse.bacc as _bacc
    from concourse import mybir as _mybir
    from concourse.bass_utils import run_bass_kernel_spmd as _run

    nc = _bacc.Bacc("TRN2", target_bir_lowering=False, num_devices=1)
    arrays, args = {}, []
    for name in _INS:
        a = _np.ascontiguousarray(inputs[name])
        arrays[f"in_{name}_dram"] = a
        args.append(nc.dram_tensor(f"in_{name}_dram", a.shape, _mybir.dt.from_np(a.dtype), kind="ExternalInput").ap())
    shape = inputs["x"].shape
    args.append(nc.dram_tensor("out_0_dram", shape, _mybir.dt.from_np(_np.dtype("float32")),
                               kind="ExternalOutput").ap())
    decoder_trunk(nc, *args)
    r = _run(nc, [arrays], core_ids=[0])
    return r.results[0]["out_0_dram"]
```

```python
import math
from contextlib import ExitStack

import numpy as np

import concourse.bass as bass
from concourse import mybir

ALU = mybir.AluOpType
ACT = mybir.ActivationFunctionType
F32 = mybir.dt.float32
F32R = mybir.dt.float32r
U32 = mybir.dt.uint32
AX_X = mybir.AxisListType.X

P = 128
LN_EPS = 1e-5
MASKED = -1e32
LOWEST = -3.0e38
RING = 8
VRING = 4


def alibi(n):
    return [float(s) for s in (2.0 ** (-8.0 * np.arange(1, n + 1) / n)).astype(np.float32)]


def decoder_trunk(nc, x, a_w_qkv, a_sinks, a_w_o, b_w_qkv, b_lambda_q1, b_lambda_k1, b_lambda_q2, b_lambda_k2,
                  b_subln_g, b_w_o, ln1_g, ln1_b, ln2_g, ln2_b, peer_w_q, peer_subkeys, peer_u, peer_v, out):
    _, SEQ, D = x.shape
    DEPTH = ln1_g.shape[0]
    A_HEADS = a_sinks.shape[1]
    HD = b_lambda_q1.shape[1]
    A_KV = (a_w_qkv.shape[2] // HD - A_HEADS) // 2
    VD = b_subln_g.shape[1]
    B_HEADS = b_w_o.shape[1] // VD
    PH, NKEYS, PHALF = peer_subkeys.shape[1], peer_subkeys.shape[3], peer_subkeys.shape[4]
    HC = 2 * PH
    TOPK = 16
    PICKS = PH * TOPK
    T = SEQ // P
    KT = D // P
    ALPHA = (2.0 * DEPTH) ** 0.25
    SCALE = HD ** -0.5
    GROUP = 512
    KK = 4
    CH = KT // KK
    BPG = GROUP // P
    POOL_KK = 3
    POOL_FROM = 1344
    assert T == 2 and D == 2048 and HD == 64 and PICKS == P and NKEYS == P and PHALF == P and DEPTH == 2
    slopes = [alibi(A_HEADS), alibi(B_HEADS)]

    LATE_PAIR = [(0, 0), (0, 1), (0, 2), (1, 0), (1, 1), (1, 2), (0, 3), (1, 3), (2, 0), (2, 1), (2, 2), (2, 3),
                 (3, 0), (3, 1), (3, 2), (3, 3)]

    def stream(l):
        if l == 0:
            cols = [A_HEADS * HD] + [g * GROUP for g in range(4)]
        else:
            cols = [c * D + h * GROUP for h in range(4) for c in range(3)]
        out = [("qkv", col, q, g) for g, col in enumerate(cols) for q in range(CH)]
        n = len(cols)
        out += [("wo", g * GROUP, q, n + g) for g, q in LATE_PAIR]
        out += [("wq", g * GROUP, q, n + 4 + g) for g in range(4) for q in range(CH)]
        return out

    STREAM = [stream(l) for l in range(DEPTH)]
    C0 = [0, len(STREAM[0])]
    G0 = [0, len(STREAM[0]) // CH]
    NCHUNKS = sum(len(s) for s in STREAM)
    QKV = [5, 12]
    JOBS = T * PICKS
    BATCHES = JOBS // RING
    TB = BATCHES // T
    VG = D // 2
    VB = (D - VG) // P
    SPREAD = 8
    assert P // SPREAD == TB
    STEPS = 16
    WQ_SLOT = [CH * (QKV[l] + 4) for l in range(DEPTH)]

    def last_chunk(l, g):
        return max(i for i, c in enumerate(STREAM[l]) if c[3] == g)

    def group_done(l, g):
        return C0[l] + last_chunk(l, g) + 1

    def dve_lows(c):
        return sum(STREAM[l][i][0] != "wq" for l in range(DEPTH) for i in range(len(STREAM[l])) if C0[l] + i < c)

    def finished(l, i):
        return [g for g in range(len(STREAM[l]) // CH) if last_chunk(l, g) == i - 1]

    def place(l, s):
        return (s % 2, s // 2) if l == 0 else ((s % 4) // 2, 2 * (s // 4) + s % 2)

    def slot_of(l, s):
        return 8 + s if l == 0 else 12 * (s // 4 + 1) + s % 4

    def step_at(l, i):
        found = [s for s in range(STEPS) if slot_of(l, s) == i]
        return found[0] if found else None

    def unit_at(l, i):
        if l == 0:
            return []
        last = 12 * 4 + 6
        return [2 * h + t for h in range(4) for t in range(T) if min(12 * (h + 1) + 7 + t, last) == i]

    def blocks_before(s):
        return sum(place(0, j)[0] + 1 for j in range(s))

    def turned(l, s):
        return blocks_before(s + 1) if l == 0 else blocks_before(STEPS) + s + 1

    with ExitStack() as ctx:
        def sem(name):
            return ctx.enter_context(nc.semaphore(name))

        base = -(-nc.sbuf_base // 64) * 64
        top_of = [0]

        def at(name, offset, shape, dt=F32):
            size = int(np.prod(shape[1:])) * 4
            top_of[0] = max(top_of[0], offset + size)
            return nc.alloc_sbuf_tensor_at(name, shape, dt, offset=base + offset)

        K = 1024
        xt = at("xt", 0, [P, T, D])
        raw = at("raw", 16 * K, [P, 2, KK, GROUP])
        w_hi = at("w_hi", 32 * K, [P, 2, KK, GROUP], F32R)
        w_lo = at("w_lo", 48 * K, [P, 2, KK, GROUP], F32R)
        xT_hi = at("xT_hi", 64 * K, [P, KT, T * P], F32R)
        xT_lo = at("xT_lo", 80 * K, [P, KT, T * P], F32R)
        oT_hi = at("oT_hi", 96 * K, [P, KT, T * P], F32R)
        oT_lo = at("oT_lo", 112 * K, [P, KT, T * P], F32R)
        qT = at("qT", 128 * K, [P, 2, BPG, T * P])
        kT = at("kT", 136 * K, [P, 2, BPG, T * P])
        vn = at("vn", 144 * K, [P, 2, T, GROUP])
        prob = at("prob", 152 * K, [P, 3, 4, 2 * P])
        pT = at("pT", 164 * K, [P, 2, 2, GROUP])
        orow = at("orow", 172 * K, [P, 2, GROUP])
        osq = at("osq", 176 * K, [P, GROUP])
        gb1 = at("gb1", 178 * K, [P, 2, D])
        skn = at("skn", 128 * K, [P, HC, PHALF])
        ring = at("ring", 96 * K, [P, RING, D])
        skT = at("skT", 160 * K, [P, HC, NKEYS])
        pqT = at("pqT", 168 * K, [P, 2, BPG, T * P])
        sc = at("sc", 176 * K, [P, 2, T, 4 * NKEYS])
        cand = at("cand", 184 * K, [P, T, 2, TOPK * TOPK])
        hot = at("hot", 188 * K, [P, 2, 2 * TOPK, TOPK])
        spread = at("spread", 16 * K, [P, T, NKEYS, P])
        onehot = at("onehot", 160 * K, [P, 2, 2, SPREAD, P])
        vring = at("vring", 176 * K, [P, VRING, VG])
        vblk = at("vblk", 144 * K, [P, VRING, D - VG])
        pick = at("pick", 192 * K, [P, 2, PICKS], U32)
        pickf = at("pickf", 193 * K, [P, 2, PICKS])
        gb2 = at("gb2", 160 * K, [P, 2, D])
        vout = at("vout", 64 * K, [P, VB, T * P])
        small_at = [194 * K]

        def small(name, shape, dt=F32):
            t = at(name, small_at[0], shape, dt)
            small_at[0] += -(-int(np.prod(shape[1:])) * 4 // 32) * 32
            return t

        ident = small("ident", [P, P])
        mask = small("mask", [P, 2, 2 * P])
        iota16 = small("iota16", [P, TOPK])
        iota_keys = small("iota_keys", [P, NKEYS])
        pickT = small("pickT", [P, 3, P])
        sink8 = small("sink8", [P, A_HEADS])
        lamv = small("lamv", [P, 4, HD])
        subg = small("subg", [P, VD])
        sm = small("sm", [P, 8])
        mx = small("mx", [P, 2, 4])
        nm = small("nm", [P, 2, 4])
        rs = small("rs", [P, 2, 4])
        sk = small("sk", [P, 2, 4])
        rd = small("rd", [P, 2, 4])
        sq = small("sq", [P, 3, 4])
        stats = small("stats", [P, T, 4, 6])
        mv = small("mv", [P, T, 4])
        top = small("top", [P, 4, TOPK])
        topi = small("topi", [P, 4, TOPK], U32)
        topf = small("topf", [P, 4, TOPK])
        best = small("best", [P, 2, TOPK])
        pos = small("pos", [P, 3, 2 * TOPK], U32)
        posf = small("posf", [P, 2, 2 * TOPK])
        key = small("key", [P, 2, 2 * TOPK])
        gsum = small("gsum", [P, 2, PH])
        idx = small("idx", [P, T, PICKS], U32)
        idxs = small("idxs", [P, 2, RING], U32)
        gate = small("gate", [P, T, PICKS])
        act8 = small("act8", [P, RING])
        act = small("act", [P, T, PICKS])
        assert base + top_of[0] <= nc.sbuf_usable_end, (base, top_of[0], nc.sbuf_usable_end)
        ps = ctx.enter_context(nc.psum_tensor("ps", [P, 8, 512], F32))

        x_in = [sem(f"x_in{t}") for t in range(T)]
        small_in = sem("small_in")
        gb_in = sem("gb_in")
        sk_in = sem("sk_in")
        w_in = [sem(f"w_in{r}") for r in range(2)]
        hi_done = sem("hi_done")
        lo_pool = sem("lo_pool")
        lo_dve = sem("lo_dve")
        w_used = sem("w_used")
        rows_in = [sem(f"rows_in{r}") for r in range(RING)]
        slot_free = sem("slot_free")
        idx_staged = sem("idx_staged")
        gathers_begun = sem("gathers_begun")
        out_done = sem("out_done")
        const_pool = sem("const_pool")
        xT_done = sem("xT_done")
        xT_top = sem("xT_top")
        xT_rest = sem("xT_rest")
        proj_free = sem("proj_free")
        k_spread = sem("k_spread")
        sc_done = sem("sc_done")
        sc_ready = sem("sc_ready")
        sc_exp = sem("sc_exp")
        prob_ready = sem("prob_ready")
        pt_done = sem("pt_done")
        pt_moved = sem("pt_moved")
        pv_done = sem("pv_done")
        pv_top = sem("pv_top")
        pv_moved = sem("pv_moved")
        sub_sq = sem("sub_sq")
        sub_rt = sem("sub_rt")
        sub_done = sem("sub_done")
        ot_done = sem("ot_done")
        ot_top = sem("ot_top")
        ot_rest = sem("ot_rest")
        lam_dot = sem("lam_dot")
        lam_exp = sem("lam_exp")
        ln_var = sem("ln_var")
        ln_root = sem("ln_root")
        ln_scaled = sem("ln_scaled")
        ln_done = sem("ln_done")
        ln_pool = sem("ln_pool")
        pool_step = sem("pool_step")
        skT_done = sem("skT_done")
        skT_moved = sem("skT_moved")
        rt_done = sem("rt_done")
        rt_moved = sem("rt_moved")
        gate_sub = sem("gate_sub")
        gate_exp = sem("gate_exp")
        routed = sem("routed")
        vrows_in = [sem(f"vrows_in{r}") for r in range(VRING)]
        vslot_free = sem("vslot_free")
        vblk_in = [sem(f"vblk_in{r}") for r in range(VRING)]
        vblk_used = sem("vblk_used")
        picks_ready = sem("picks_ready")
        pickT_done = sem("pickT_done")
        pickT_moved = sem("pickT_moved")
        onehot_ready = sem("onehot_ready")
        spread_done = sem("spread_done")
        spread_moved = sem("spread_moved")
        gathered = sem("gathered")
        vout_moved = sem("vout_moved")
        vout_turned = sem("vout_turned")
        dots_kept = sem("dots_kept")
        gelu_done = sem("gelu_done")
        dve_step = sem("dve_step")

        W = {("qkv", 0): a_w_qkv[0], ("qkv", 1): b_w_qkv[0], ("wo", 0): a_w_o[0], ("wo", 1): b_w_o[0]}
        W.update({("wq", l): peer_w_q[l] for l in range(DEPTH)})

        def ln_finished(eng, n):
            eng.wait_ge(ln_done, n + 1)
            eng.wait_ge(ln_pool, n + 1)

        UNITS = [(j, t) for j in range(PH // 2) for t in range(T)]
        DOTS = [(j, t) for t in range(T) for j in range(PH // 2)]
        UB = 2 * TOPK // RING

        def x_bank(n, t):
            return 4 * (t if n % 2 == 0 else 1 - t)

        def gain_shift(eng, dst, g, b, l):
            for j, v in enumerate((g, b)):
                eng.dma_start(dst[:, j, :], v[l:l + 1, :].broadcast_to([P, D])).then_inc(gb_in, 16)

        def vsum(t):
            lo = 6 - 2 * t
            return ps[:, lo:lo + 2, :].rearrange("p b n -> p (b n)")

        block = ctx.enter_context(nc.Block())

        @block.sync
        def _(sp):
            for t in range(T):
                sp.dma_start(xt[:, t, :], x[0, t * P:(t + 1) * P, :]).then_inc(x_in[t], 16)

            for l in range(DEPTH):
                for i, (name, col, q, _g) in enumerate(STREAM[l]):
                    c = C0[l] + i
                    if c >= 2:
                        sp.wait_ge(hi_done, c - 1)
                        sp.wait_ge(lo_pool, c - 1)
                        if dve_lows(c - 1) > dve_lows(c - 2):
                            sp.wait_ge(lo_dve, dve_lows(c - 1))
                    src = W[name, l].rearrange("(q k p) n -> q p k n", p=P, k=KK)[q][:, :, col:col + GROUP]
                    sp.dma_start(raw[:, c % 2], src).then_inc(w_in[c % 2], 16)
                    if i == 8:
                        if l:
                            ln_finished(sp, 2 * T * l - 1)
                        gain_shift(sp, gb1, ln1_g, ln1_b, l)
                    if i == WQ_SLOT[l] - 7:
                        sp.wait_ge(pv_moved, STEPS * (l + 1))
                        sp.dma_start(skn[:], peer_subkeys[l].rearrange("h c k d -> k (h c) d")).then_inc(sk_in, 16)
                sp.wait_ge(slot_free, RING + JOBS * (l + 1))
                experts = peer_v.rearrange("l e d -> (l e) d")
                with sp.Fori(0, NKEYS // VRING) as it:
                    for r in range(VRING):
                        sp.wait_ge(vblk_used, it * VRING + l * NKEYS + r + 1)
                        sp.dma_start(vblk[:, r, :], experts[bass.ds(it * (VRING * P) + (l * NKEYS + r) * P, P), VG:D]
                                     ).then_inc(vblk_in[r], 16)
                sp.wait_ge(vblk_used, NKEYS * (l + 1) + VRING)
            for t in range(T):
                ln_finished(sp, 2 * T * (DEPTH - 1) + T + t)
                sp.dma_start(out[0, t * P:(t + 1) * P, :], xt[:, t, :]).then_inc(out_done, 16)
            sp.wait_ge(out_done, 16 * T)

        @block.gpsimd
        def _(pool):
            pool.memset(ident[:], 0.0).then_inc(const_pool, 1)
            for m in range(2):
                pool.iota(mask[:, m, :], [[1, 2 * P]], base=-P, channel_multiplier=-1,
                          allow_small_or_imprecise_dtypes=True).then_inc(const_pool, 1)
            pool.iota(iota16[:], [[1, TOPK]], base=0, channel_multiplier=0,
                      allow_small_or_imprecise_dtypes=True).then_inc(const_pool, 1)
            pool.iota(iota_keys[:], [[1, NKEYS]], base=0, channel_multiplier=0,
                      allow_small_or_imprecise_dtypes=True).then_inc(const_pool, 1)
            pool.wait_ge(const_pool, 5)
            pool.affine_select(out=ident[:], in_=ident[:], compare_op=ALU.not_equal, fill=1.0, base=0,
                               pattern=[[-1, P]], channel_multiplier=1).then_inc(const_pool, 1)
            for m in range(2):
                pool.affine_select(out=mask[:, m, :], in_=mask[:, m, :], compare_op=ALU.is_ge, fill=MASKED, base=P,
                                   pattern=[[-1, 2 * P]], channel_multiplier=1).then_inc(const_pool, 1)
            pool.wait_ge(const_pool, 8)
            pool.affine_select(out=mask[:, 0, :], in_=mask[:, 0, :], compare_op=ALU.is_ge, fill=MASKED, base=-1,
                               pattern=[[1, 2 * P]], channel_multiplier=-1).then_inc(const_pool, 1)
            steps = [0]

            def low_part(l, i):
                c = C0[l] + i
                share = KK if STREAM[l][i][0] == "wq" else POOL_KK
                pool.wait_ge(hi_done, c + 1)
                if c >= 2:
                    pool.wait_ge(w_used, c - 1)
                r = c % 2
                pool.tensor_tensor(w_lo[:, r, 0:share, :], raw[:, r, 0:share, :],
                                   w_hi[:, r, 0:share, :].bitcast(F32), ALU.subtract).then_inc(lo_pool, 1)

            def norm_share(n, t, gb):
                pool.wait_ge(ln_scaled, n + 1)
                pool.wait_ge(gb_in, 32 * (n // T + 1))
                xs = xt[:, t, POOL_FROM:D]
                pool.tensor_tensor(xs, xs, gb[:, 0, POOL_FROM:D], ALU.mult).then_inc(pool_step, 1)
                steps[0] += 1
                pool.wait_ge(pool_step, steps[0])
                pool.tensor_tensor(xs, xs, gb[:, 1, POOL_FROM:D], ALU.add).then_inc(ln_pool, 1)

            def gather_u(t, col, batch, half, it=0, stride=0):
                pool.tensor_copy(idxs[:, half, :], idx[:, t, bass.ds(it * (stride * RING) + col, RING)]
                                 ).then_inc(idx_staged, 1)
                pool.wait_ge(idx_staged, it * stride + batch // BATCHES * BATCHES + batch + 1)
                for r in range(RING):
                    pool.wait_ge(slot_free, it * (stride * RING) + batch * RING + r + 1)
                    pool.sem_inc(gathers_begun, 1)
                    pool.indirect_dma_start(
                        out=ring[:, r, :], out_offset=None, in_=peer_u.rearrange("l e d -> (l e) d"),
                        in_offset=bass.IndirectOffsetOnAxis(ap=idxs[:, half, r:r + 1], axis=0),
                    ).then_inc(rows_in[r], 16)

            def gather_v(l, t, half, it):
                picks = idx[:, t, bass.ds(it * (2 * RING) + half * RING, RING)]
                pool.tensor_tensor(idxs[:, half, :], picks, picks, ALU.add).then_inc(idx_staged, 1)
                pool.wait_ge(idx_staged, it * 2 + (2 * l + 1) * BATCHES + t * TB + half + 1)
                for r in range(RING):
                    pool.wait_ge(vslot_free, it * (2 * RING) + l * JOBS + t * PICKS + half * RING + r + 1)
                    pool.sem_inc(gathers_begun, 1)
                    pool.indirect_dma_start(
                        out=vring[:, r % VRING, :], out_offset=None,
                        in_=peer_v.rearrange("l e (h d) -> (l e h) d", d=VG),
                        in_offset=bass.IndirectOffsetOnAxis(ap=idxs[:, half, r:r + 1], axis=0),
                    ).then_inc(vrows_in[r % VRING], 16)

            for l in range(DEPTH):
                b0 = l * BATCHES

                def unit_routed(n):
                    j, t = DOTS[n]
                    pool.wait_ge(routed, len(UNITS) * l + UNITS.index((j, t)) + 1)

                def early(b):
                    j, t = DOTS[b // UB]
                    if b % UB == 0:
                        unit_routed(b // UB)
                    gather_u(t, 2 * TOPK * j + (b % UB) * RING, b0 + b, b % 2)

                for i in range(1 if l else 0, len(STREAM[l])):
                    low_part(l, i)
                    if i == WQ_SLOT[l]:
                        for t in range(T):
                            norm_share(2 * T * l + t, t, gb1)
                    if i == WQ_SLOT[l] + 7:
                        early(0)
                for b in range(1, UB):
                    early(b)
                for n, (j, t) in enumerate(DOTS[1:], 1):
                    unit_routed(n)
                    with pool.Fori(0, UB // 2) as it:
                        for half in range(2):
                            gather_u(t, 2 * TOPK * j + half * RING, b0 + n * UB + half, half, it, 2)
                for t in range(T):
                    with pool.Fori(0, TB // 2) as it:
                        for half in range(2):
                            gather_v(l, t, half, it)
                norm_share(2 * T * l + T, 0, gb2)
                if l + 1 < DEPTH:
                    low_part(l + 1, 0)
                norm_share(2 * T * l + T + 1, 1, gb2)

        @block.scalar
        def _(a):
            a.dma_start(sink8[:], a_sinks[0:1, :].broadcast_to([P, A_HEADS])).then_inc(small_in, 16)
            for j, v in enumerate((b_lambda_q1, b_lambda_k1, b_lambda_q2, b_lambda_k2)):
                a.dma_start(lamv[:, j, :], v[0:1, :].broadcast_to([P, HD])).then_inc(small_in, 16)
            a.dma_start(subg[:], b_subln_g[0:1, :].broadcast_to([P, VD])).then_inc(small_in, 16)

            def high_part(c):
                a.wait_ge(w_in[c % 2], 16 * (c // 2 + 1))
                if c >= 2:
                    a.wait_ge(w_used, c - 1)
                a.copy(w_hi[:, c % 2], raw[:, c % 2]).then_inc(hi_done, 1)

            def top_xT(n):
                for t in range(T):
                    for b in range(4):
                        a.wait_ge(xT_done, (n * T + t) * 4 + b + 1)
                        a.copy(xT_hi[:, 4 * b:4 * b + 4, t * P:(t + 1) * P],
                               ps[:, x_bank(n, t) + b, :].rearrange("p (k n) -> p k n", n=P)).then_inc(xT_top, 1)

            def root(n):
                a.wait_ge(ln_var, n + 1)
                a.activation(mv[:, n % T, 2:3], mv[:, n % T, 1:2], ACT.Sqrt).then_inc(ln_root, 1)

            def move_group(l, g):
                if QKV[l] <= g < QKV[l] + 4:
                    return
                G = G0[l] + g
                lo = 2 * (G % 2)
                a.wait_ge(w_used, group_done(l, g))
                if g >= QKV[l] + 4:
                    j = g - QKV[l] - 4
                    if j >= 2:
                        a.wait_ge(rt_done, len(UNITS) * l + T * (j - 1))
                    dst = pqT[:, j % 2]
                elif l == 0 and g == 0:
                    a.copy(kT[:, 1, 0:2, :], ps[:, 0, :].rearrange("p (k n) -> p k n", n=T * P))
                    a.copy(vn[:, 0, :, 0:A_KV * HD], ps[:, 1, :].rearrange("p (t n) -> p t n", t=T)
                           ).then_inc(proj_free, 1)
                    a.wait_ge(proj_free, 1)
                    for src in range(2):
                        for dst in range(2):
                            a.dma_start(kT[HD * dst:HD * (dst + 1), 0, src::2, :],
                                        kT[HD * src:HD * (src + 1), 1, 0:2, :]).then_inc(k_spread, 16)
                    return
                elif l == 0:
                    if g - 1 >= 2:
                        a.wait_ge(sc_done, 4 * (g - 2))
                    dst = qT[:, (g - 1) % 2]
                else:
                    h = g // 3
                    if h >= 2:
                        a.wait_ge(pv_done, STEPS + 4 * (h - 1))
                    if g % 3 == 2:
                        for t in range(T):
                            last = a.copy(vn[:, h % 2, t, :], ps[:, lo + t, :])
                        last.then_inc(proj_free, 1)
                        return
                    dst = (qT if g % 3 == 0 else kT)[:, h % 2]
                for b in range(2):
                    last = a.copy(dst[:, 2 * b:2 * b + 2, :], ps[:, lo + b, :].rearrange("p (k n) -> p k n", n=T * P))
                last.then_inc(proj_free, 1)

            def exps(l, s):
                t, _ = place(l, s)
                w = P * (t + 1)
                a.wait_ge(sc_ready, l * STEPS + s + 1)
                for m in range(4):
                    last = a.activation(prob[:, s % 3, m, 0:w], prob[:, s % 3, m, 0:w], ACT.Exp,
                                        bias=nm[:, s % 2, m:m + 1], scale=SCALE, accum_out=rs[:, s % 2, m:m + 1])
                if l == 0:
                    last = a.activation(sk[:, s % 2, :], sk[:, s % 2, :], ACT.Exp)
                last.then_inc(sc_exp, 1)

            def move_turned(l, s, b):
                t, _ = place(l, s)
                n = turned(l, s) - (t - b if l == 0 else 0)
                a.wait_ge(pt_done, n)
                if s >= 2 and b == 0:
                    a.wait_ge(pv_done, l * STEPS + s - 1)
                if l == 0:
                    a.copy(pT[:, s % 2, b, :], ps[:, 6, :]).then_inc(pt_moved, 1)
                else:
                    a.copy(pT[:, s % 2, 0, 0:2 * P * (t + 1)], ps[:, 6, 0:2 * P * (t + 1)]).then_inc(pt_moved, 1)

            def unit(u):
                h, t = u // T, u % T
                a.wait_ge(ot_done, u + 1)
                a.copy(oT_hi[:, 4 * h:4 * h + 4, t * P:(t + 1) * P], ps[:, 7, :].rearrange("p (k n) -> p k n", n=P)
                       ).then_inc(ot_top, 1)

            def unit_root(u):
                a.wait_ge(sub_sq, u + 1)
                a.activation(sq[:, 1, :], sq[:, 0, :], ACT.Sqrt).then_inc(sub_rt, 1)

            def route_scores(l, j):
                for t in range(T):
                    a.wait_ge(rt_done, len(UNITS) * l + T * j + t + 1)
                    if j >= 2:
                        a.wait_ge(routed, len(UNITS) * l + T * (j - 2) + t + 1)
                    a.copy(sc[:, j % 2, t, :], ps[:, 4 + 2 * (j % 2) + t, :]).then_inc(rt_moved, 1)

            def move_spread(l, t):
                a.wait_ge(pickT_done, T * l + t + 1)
                a.copy(pickT[:], ps[:, 4, 0:3 * P].rearrange("p (k n) -> p k n", n=P)).then_inc(pickT_moved, 1)
                with a.Fori(0, TB) as it:
                    for half in range(2):
                        a.wait_ge(spread_done, it * 2 + 2 * TB * (T * l + t) + half + 1 + 4)
                        a.copy(spread[:, t, :, bass.ds(it * SPREAD + 4 * half, 4)],
                               ps[:, 4 + half, :].rearrange("p (q k) -> p k q", q=4)).then_inc(spread_moved, 1)

            a.sem_inc(spread_moved, 2)
            high_part(0)
            for l in range(DEPTH):
                if l == 1:
                    a.wait_ge(lam_dot, 2)
                    a.activation(sm[:, 2:4], sm[:, 0:2], ACT.Exp).then_inc(lam_exp, 1)
                top_xT(2 * l)
                for i in range(len(STREAM[l])):
                    if i == WQ_SLOT[l]:
                        for b in range(4):
                            a.wait_ge(skT_done, l * 4 + b + 1)
                            a.copy(skT[:, 4 * b:4 * b + 4, :], ps[:, 4 + b, :].rearrange("p (k n) -> p k n", n=P)
                                   ).then_inc(skT_moved, 1)
                        for t in range(T):
                            root(2 * T * l + t)
                        top_xT(2 * l + 1)
                    for g in finished(l, i):
                        move_group(l, g)
                    if i + 1 < len(STREAM[l]):
                        high_part(C0[l] + i + 1)
                    s3, s2, s0 = step_at(l, i - 3), step_at(l, i - 2), step_at(l, i)
                    if s3 is not None and l == 0:
                        t, hg = place(l, s3)
                        a.wait_ge(pv_done, s3 + 1)
                        a.copy(oT_hi[:, 2 * hg:2 * hg + 2, t * P:(t + 1) * P],
                               ps[:, 7, 0:2 * P].rearrange("p (j q) -> p j q", q=P)).then_inc(pv_top, 1)
                    if s3 is not None and l == 1 and s3 % 2 == 1:
                        unit_root(s3 // 2)
                    for u in unit_at(l, i):
                        unit(u)
                    if s2 is not None:
                        for b in range(place(l, s2)[0] + 1 if l == 0 else 1):
                            move_turned(l, s2, b)
                    if s0 is not None:
                        exps(l, s0)
                    j = i - WQ_SLOT[l]
                    if j > 0 and j % CH == 0:
                        route_scores(l, j // CH - 1)
                for g in finished(l, len(STREAM[l])):
                    move_group(l, g)
                route_scores(l, PH // 2 - 1)
                for t in range(T):
                    a.wait_ge(gate_sub, len(UNITS) * (l + 1) - T + t + 1)
                    a.activation(gate[:, t, :], gate[:, t, :], ACT.Exp).then_inc(gate_exp, 1)
                for t in range(T):
                    a.wait_ge(dots_kept, l * BATCHES + (t + 1) * TB + 1)
                    a.activation(act[:, t, :], act[:, t, :], ACT.Gelu).then_inc(gelu_done, 1)
                    move_spread(l, t)
                a.wait_ge(spread_done, 2 * T * TB * (l + 1) + 4)
                gain_shift(a, gb2, ln2_g, ln2_b, l)
                a.wait_ge(vblk_used, NKEYS * (l + 1) + VRING)
                for b in range(4):
                    a.copy(vout[:, 2 * b:2 * b + 2, :], ps[:, b, :].rearrange("p (k n) -> p k n", n=T * P)
                           ).then_inc(vout_moved, 1)
                if l + 1 < DEPTH:
                    high_part(C0[l + 1])
                for t in range(T):
                    root(2 * T * l + T + t)

        @block.tensor
        def _(pe):
            def transpose_x(n):
                for t in range(T):
                    if n == 0:
                        pe.wait_ge(x_in[t], 16)
                        pe.wait_ge(const_pool, 6)
                    else:
                        ln_finished(pe, T * (n - 1) + t)
                    for k in range(KT):
                        b = x_bank(n, t) + k // 4
                        last = pe.transpose(ps[:, b, (k % 4) * P:(k % 4 + 1) * P], xt[:, t, k * P:(k + 1) * P],
                                            ident[:])
                        if k % 4 == 3:
                            last.then_inc(xT_done, 1)
                pe.wait_ge(xT_top, (n + 1) * 4 * T)
                pe.wait_ge(xT_rest, (n + 1) * 4 * T)

            def subkeys(l):
                pe.wait_ge(sk_in, 16 * (l + 1))
                for k in range(HC):
                    last = pe.transpose(ps[:, 4 + k // 4, (k % 4) * P:(k % 4 + 1) * P], skn[:, k, :], ident[:])
                    if k % 4 == 3:
                        last.then_inc(skT_done, 1)
                pe.wait_ge(skT_moved, 4 * (l + 1))

            def product(out_ap, stationary, moving, start, stop):
                (s_hi, s_lo), (m_hi, m_lo) = stationary, moving
                pe.matmul(out_ap, s_hi, m_hi, start=start, stop=False, skip_group_check=True)
                pe.matmul(out_ap, s_hi, m_lo, start=False, stop=False, skip_group_check=True)
                return pe.matmul(out_ap, s_lo, m_hi, start=False, stop=stop, skip_group_check=True)

            def half_chunk(l, i, half):
                name, _col, q, g = STREAM[l][i]
                c, G = C0[l] + i, G0[l] + g
                r = c % 2
                if half == 0:
                    if q == 0 and G >= 2:
                        pe.wait_ge(proj_free, G - 1)
                    pe.wait_ge(hi_done, c + 1)
                    pe.wait_ge(lo_pool, c + 1)
                    if dve_lows(c + 1) > dve_lows(c):
                        pe.wait_ge(lo_dve, dve_lows(c + 1))
                act_hi, act_lo = (oT_hi, oT_lo) if name == "wo" else (xT_hi, xT_lo)
                by_rows = name == "wo" or (name == "qkv" and l == 1 and g % 3 == 2)
                lo = 2 * (G % 2)
                for kk in range(2 * half, 2 * half + 2):
                    k = q * KK + kk
                    stop = k == KT - 1
                    moving = (act_hi[:, k, :], act_lo[:, k, :])

                    def rows_of(t):
                        return tuple(x_[:, k, t * P:(t + 1) * P] for x_ in (act_hi, act_lo))

                    def cols(c0, n):
                        return tuple(w[:, r, kk, c0:c0 + n] for w in (w_hi, w_lo))

                    if name == "qkv" and l == 0 and g == 0:
                        for b in range(2):
                            product(ps[:, 0, b * 256:(b + 1) * 256], cols(b * P, P), moving, k == 0 and b == 0, stop)
                        for t in range(T):
                            last = product(ps[:, 1, t * 256:(t + 1) * 256], rows_of(t), cols(A_KV * HD, A_KV * HD),
                                           k == 0 and t == 0, stop)
                    elif by_rows:
                        for t in range(T):
                            last = product(ps[:, lo + t, :], rows_of(t), cols(0, GROUP), k == 0, stop)
                    else:
                        for b in range(BPG):
                            last = product(ps[:, lo + b // 2, (b % 2) * 256:(b % 2) * 256 + 256], cols(b * P, P),
                                           moving, k == 0 and b % 2 == 0, stop)
                if half:
                    last.then_inc(w_used, 1)

            def scores(l, s):
                n = l * STEPS + s
                t, hg = place(l, s)
                w = P * (t + 1)
                buf = (s // 4) % 2
                pe.wait_ge(proj_free, G0[l] + (s // 4 + 2 if l == 0 else 3 * (s // 4) + 3))
                if l == 0:
                    pe.wait_ge(k_spread, 64)
                if n:
                    pe.wait_ge(sc_ready, n)
                for m in range(4):
                    half = slice(HD * (m % 2), HD * (m % 2) + HD)
                    blk = 2 * (hg % 2) + m // 2
                    keys = kT[half, 0, hg // 2, 0:w] if l == 0 else kT[half, buf, blk, 0:w]
                    last = pe.matmul(ps[:, 4 + m % 2, (m // 2) * 256:(m // 2) * 256 + w],
                                     qT[half, buf, blk, t * P:(t + 1) * P], keys, start=True, stop=True)
                last.then_inc(sc_done, 1)

            def turn(l, s, b):
                t, _ = place(l, s)
                done = turned(l, s) - (t - b if l == 0 else 0)
                pe.wait_ge(prob_ready, l * STEPS + s + 1)
                if done > 1:
                    pe.wait_ge(pt_moved, done - 1)
                if l == 0:
                    pairs = [(j, m, b) for j, m in enumerate((0, 2, 1, 3))]
                else:
                    pairs = [(2 * bb + j, 2 * j, bb) for bb in range(t + 1) for j in range(2)]
                for col, m, bb in pairs:
                    last = pe.transpose(ps[:, 6, col * P:(col + 1) * P], prob[:, s % 3, m, bb * P:(bb + 1) * P],
                                        ident[:])
                last.then_inc(pt_done, 1)

            def values(l, s):
                n = l * STEPS + s
                t, hg = place(l, s)
                pe.wait_ge(pt_moved, turned(l, s))
                if n:
                    pe.wait_ge(pv_moved, n)
                if l == 1:
                    pe.wait_ge(proj_free, G0[l] + 3 * (s // 4) + 3)
                    if s // 4:
                        pe.wait_ge(ot_rest, 2 * (s // 4))
                for j in range(2):
                    for b in range(t + 1):
                        flags = dict(start=(b == 0), stop=(b == t))
                        if l == 0:
                            last = pe.matmul(ps[HD * j:HD * j + HD, 7, 0:2 * P],
                                             vn[:, 0, b, (hg // 2) * HD:(hg // 2 + 1) * HD],
                                             pT[:, s % 2, b, 2 * j * P:2 * (j + 1) * P], **flags)
                        else:
                            h = 2 * (s % 2) + j
                            last = pe.matmul(ps[:, 7, j * VD:(j + 1) * VD],
                                             pT[:, s % 2, 0, (2 * b + j) * P:(2 * b + j + 1) * P],
                                             vn[:, (s // 4) % 2, b, h * VD:(h + 1) * VD], **flags)
                last.then_inc(pv_done, 1)

            def unit(u):
                pe.wait_ge(sub_done, u + 1)
                pe.wait_ge(pv_moved, STEPS + 4 * (u // T + 1))
                if u:
                    pe.wait_ge(ot_rest, u)
                for k in range(4):
                    last = pe.transpose(ps[:, 7, k * P:(k + 1) * P], orow[:, u % 2, k * P:(k + 1) * P], ident[:])
                last.then_inc(ot_done, 1)

            def route_products(l, j):
                pe.wait_ge(proj_free, G0[l] + QKV[l] + 4 + j + 1)
                if j >= 2:
                    pe.wait_ge(rt_moved, len(UNITS) * l + T * (j - 1))
                for t in range(T):
                    for b in range(BPG):
                        last = pe.matmul(ps[:, 4 + 2 * (j % 2) + t, b * P:(b + 1) * P],
                                         pqT[:, j % 2, b, t * P:(t + 1) * P], skT[:, 4 * j + b, :],
                                         start=True, stop=True)
                    last.then_inc(rt_done, 1)

            def spread_weights(l, t):
                pe.wait_ge(picks_ready, T * l + t + 1)
                for n, rows in enumerate((pickf[:, 0, :], pickf[:, 1, :], act[:, t, :])):
                    last = pe.transpose(ps[:, 4, n * P:(n + 1) * P], rows, ident[:])
                last.then_inc(pickT_done, 1)
                g0 = TB * (T * l + t)
                with pe.Fori(0, TB // 2) as it:
                    for buf in range(2):
                        for half in range(2):
                            pe.wait_ge(onehot_ready, it * 4 + 2 * (g0 + buf) + half + 1)
                            pe.wait_ge(spread_moved, it * 4 + 2 * (g0 + buf) + half + 1)
                            for q in range(4):
                                last = pe.matmul(ps[:, 4 + half, q * P:(q + 1) * P],
                                                 onehot[:, buf, 0, 4 * half + q, :],
                                                 onehot[:, buf, 1, 4 * half + q, :], start=True, stop=True)
                            last.then_inc(spread_done, 1)

            def all_experts(l):
                pe.wait_ge(spread_moved, 2 * TB * T * (l + 1) + 2)

                def expert_block(r, at_, it, first=False):
                    pe.wait_ge(vblk_in[r], it * 16 + 16 * (l * (NKEYS // VRING) + 1))
                    for c in range(VB):
                        last = pe.matmul(ps[:, c // 2, (c % 2) * T * P:(c % 2 + 1) * T * P],
                                         vblk[:, r, c * P:(c + 1) * P], spread[:, :, at_, :],
                                         start=first and c % 2 == 0, stop=False,
                                         skip_group_check=True)
                    last.then_inc(vblk_used, 1)

                for r in range(VRING):
                    expert_block(r, slice(r, r + 1), 0, first=(r == 0))
                with pe.Fori(1, NKEYS // VRING) as it:
                    for r in range(VRING):
                        expert_block(r, bass.ds(it * VRING + r, 1), it)
                pe.wait_ge(vout_moved, 4 * (l + 1))
                for t in range(T):
                    pe.wait_ge(gathered, T * l + t + 1)
                    for c in range(VB):
                        last = pe.transpose(vsum(t)[:, c * P:(c + 1) * P], vout[:, c, t * P:(t + 1) * P], ident[:])
                    last.then_inc(vout_turned, 1)

            pe.sem_inc(spread_done, 4)
            pe.sem_inc(vblk_used, VRING)
            for l in range(DEPTH):
                transpose_x(2 * l)
                for i in range(len(STREAM[l])):
                    if i == WQ_SLOT[l]:
                        subkeys(l)
                        transpose_x(2 * l + 1)
                    s3, s2, s0 = step_at(l, i - 3), step_at(l, i - 2), step_at(l, i)
                    if s3 is not None:
                        values(l, s3)
                    for u in unit_at(l, i):
                        unit(u)
                    if s2 is not None:
                        turn(l, s2, 0)
                    if STREAM[l][i][0] == "wo":
                        if l == 0:
                            pe.wait_ge(pv_moved, 4 * (STREAM[l][i][2] + 1))
                        else:
                            pe.wait_ge(ot_rest, T * (STREAM[l][i][2] + 1))
                    half_chunk(l, i, 0)
                    if s2 is not None and l == 0 and place(l, s2)[0]:
                        turn(l, s2, 1)
                    if s0 is not None:
                        scores(l, s0)
                    j = i - WQ_SLOT[l]
                    if j > 0 and j % CH == 0:
                        route_products(l, j // CH - 1)
                    half_chunk(l, i, 1)
                route_products(l, PH // 2 - 1)
                for t in range(T):
                    spread_weights(l, t)
                all_experts(l)

        @block.vector
        def _(v):
            own = [0]

            def step(ins):
                ins.then_inc(dve_step, 1)
                own[0] += 1
                v.wait_ge(dve_step, own[0])

            v.sem_inc(slot_free, RING)
            v.sem_inc(vslot_free, VRING)
            v.sem_inc(dots_kept, 1)

            def low_part(l, i):
                if STREAM[l][i][0] == "wq":
                    return
                c = C0[l] + i
                v.wait_ge(hi_done, c + 1)
                if c >= 2:
                    v.wait_ge(w_used, c - 1)
                v.tensor_tensor(w_lo[:, c % 2, POOL_KK:KK, :], raw[:, c % 2, POOL_KK:KK, :],
                                w_hi[:, c % 2, POOL_KK:KK, :].bitcast(F32), ALU.subtract).then_inc(lo_dve, 1)

            def rest_xT(n):
                for t in range(T):
                    for b in range(4):
                        v.wait_ge(xT_top, (n * T + t) * 4 + b + 1)
                        at_ = (slice(None), slice(4 * b, 4 * b + 4), slice(t * P, (t + 1) * P))
                        v.tensor_tensor(xT_lo[at_], ps[:, x_bank(n, t) + b, :].rearrange("p (k n) -> p k n", n=P),
                                        xT_hi[at_].bitcast(F32), ALU.subtract).then_inc(xT_rest, 1)

            def layer_norm(n, t, gb):
                step(v.bn_aggr(mv[:, t, 0:2], stats[:, t].rearrange("p a b -> p (a b)")))
                v.tensor_scalar(mv[:, t, 1:2], mv[:, t, 1:2], LN_EPS, None, ALU.add).then_inc(ln_var, 1)
                v.wait_ge(ln_root, n + 1)
                step(v.reciprocal(mv[:, t, 3:4], mv[:, t, 2:3]))
                ins = v.tensor_scalar(xt[:, t, :], xt[:, t, :], mv[:, t, 0:1], mv[:, t, 3:4], ALU.subtract, ALU.mult)
                ins.then_inc(ln_scaled, 1)
                v.wait_ge(ln_scaled, n + 1)
                v.wait_ge(gb_in, 32 * (n // T + 1))
                cols = POOL_FROM
                step(v.tensor_tensor(xt[:, t, 0:cols], xt[:, t, 0:cols], gb[:, 0, 0:cols], ALU.mult))
                v.tensor_tensor(xt[:, t, 0:cols], xt[:, t, 0:cols], gb[:, 1, 0:cols], ALU.add).then_inc(ln_done, 1)

            def residual(l, g):
                G, c0 = G0[l] + g, (g - QKV[l]) * GROUP
                v.wait_ge(w_used, group_done(l, g))
                for t in range(T):
                    xs = xt[:, t, c0:c0 + GROUP]
                    last = v.scalar_tensor_tensor(out=xs, in0=xs, scalar=ALPHA, in1=ps[:, 2 * (G % 2) + t, :],
                                                  op0=ALU.mult, op1=ALU.add)
                last.then_inc(proj_free, 1)
                v.wait_ge(proj_free, G + 1)
                for t in range(T):
                    last = v.bn_stats(stats[:, t, g - QKV[l], :], xt[:, t, c0:c0 + GROUP])
                step(last)

            def bias(l, s):
                n = l * STEPS + s
                t, hg = place(l, s)
                w = P * (t + 1)
                v.wait_ge(sc_done, n + 1)
                if s >= 3:
                    v.wait_ge(pt_done, turned(l, s - 3))
                for m in range(4):
                    slope = slopes[0][4 * hg + m] if l == 0 else slopes[1][2 * hg + m // 2]
                    last = v.scalar_tensor_tensor(
                        out=prob[:, s % 3, m, 0:w], in0=mask[:, l, 2 * P - w:2 * P], scalar=slope / SCALE,
                        in1=ps[:, 4 + m % 2, (m // 2) * 256:(m // 2) * 256 + w], op0=ALU.mult, op1=ALU.add)
                step(last)
                mx_s, nm_s, sk_s = mx[:, s % 2, :], nm[:, s % 2, :], sk[:, s % 2, :]
                step(v.tensor_reduce(mx_s, prob[:, s % 3, :, 0:w], AX_X, ALU.max))
                if l == 0:
                    sinks = sink8[:, 4 * hg:4 * hg + 4]
                    step(v.tensor_tensor(mx_s, mx_s, sinks, ALU.max))
                    v.tensor_tensor(sk_s, sinks, mx_s, ALU.subtract)
                    step(v.tensor_scalar(nm_s, mx_s, -SCALE, None, ALU.mult))
                    v.tensor_scalar(sk_s, sk_s, SCALE, None, ALU.mult).then_inc(sc_ready, 1)
                else:
                    v.tensor_scalar(nm_s, mx_s, -SCALE, None, ALU.mult).then_inc(sc_ready, 1)

            def norm(l, s):
                t, _ = place(l, s)
                w = P * (t + 1)
                rd_s, p = rd[:, s % 2, :], prob[:, s % 3]
                v.wait_ge(sc_exp, l * STEPS + s + 1)
                if l == 0:
                    step(v.tensor_tensor(rd_s, rs[:, s % 2, :], sk[:, s % 2, :], ALU.add))
                    step(v.reciprocal(rd_s, rd_s))
                    for m in range(4):
                        last = v.tensor_scalar(p[:, m, 0:w], p[:, m, 0:w], rd_s[:, m:m + 1], None, ALU.mult)
                else:
                    step(v.reciprocal(rd_s, rs[:, s % 2, :]))
                    step(v.tensor_scalar(rd_s[:, 1:4:2], rd_s[:, 1:4:2], sm[:, 5:6], None, ALU.mult))
                    for m in (1, 3):
                        last = v.tensor_scalar(p[:, m, 0:w], p[:, m, 0:w], rd_s[:, m:m + 1], None, ALU.mult)
                    step(last)
                    for m in (0, 2):
                        last = v.scalar_tensor_tensor(out=p[:, m, 0:w], in0=p[:, m, 0:w], scalar=rd_s[:, m:m + 1],
                                                      in1=p[:, m + 1, 0:w], op0=ALU.mult, op1=ALU.add)
                last.then_inc(prob_ready, 1)

            def move(l, s):
                t, hg = place(l, s)
                if l == 0:
                    v.wait_ge(pv_top, s + 1)
                    at_ = (slice(None), slice(2 * hg, 2 * hg + 2), slice(t * P, (t + 1) * P))
                    v.tensor_tensor(oT_lo[at_], ps[:, 7, 0:2 * P].rearrange("p (j q) -> p j q", q=P),
                                    oT_hi[at_].bitcast(F32), ALU.subtract).then_inc(pv_moved, 1)
                else:
                    u = s // 2
                    v.wait_ge(pv_done, STEPS + s + 1)
                    if s % 2 == 0 and u >= 2:
                        v.wait_ge(ot_done, u - 1)
                    v.tensor_copy(orow[:, u % 2, (s % 2) * 2 * VD:(s % 2 + 1) * 2 * VD], ps[:, 7, 0:2 * VD]
                                  ).then_inc(pv_moved, 1)

            def sub_norm(l, u):
                li = 0.8 - 0.6 * math.exp(-0.3 * l)
                o = orow[:, u % 2, :]
                o3 = o.rearrange("p (h e) -> p h e", e=VD)
                v.wait_ge(pv_moved, STEPS + 2 * u + 2)
                step(v.tensor_tensor(osq[:], o, o, ALU.mult))
                step(v.tensor_reduce(sq[:, 0, :], osq[:].rearrange("p (h e) -> p h e", e=VD), AX_X, ALU.add))
                v.tensor_scalar(sq[:, 0, :], sq[:, 0, :], 1.0 / VD, LN_EPS, ALU.mult, ALU.add).then_inc(sub_sq, 1)
                v.wait_ge(sub_rt, u + 1)
                step(v.reciprocal(sq[:, 2, :], sq[:, 1, :]))
                step(v.tensor_scalar(sq[:, 2, :], sq[:, 2, :], 1.0 - li, None, ALU.mult))
                step(v.tensor_tensor(o3, o3, sq[:, 2, :].unsqueeze(2).broadcast_to([P, 4, VD]), ALU.mult))
                v.tensor_tensor(o3, o3, subg[:].unsqueeze(1).broadcast_to([P, 4, VD]), ALU.mult).then_inc(sub_done, 1)

            def unit_rest(u):
                h, t = u // T, u % T
                v.wait_ge(ot_top, u + 1)
                at_ = (slice(None), slice(4 * h, 4 * h + 4), slice(t * P, (t + 1) * P))
                v.tensor_tensor(oT_lo[at_], ps[:, 7, :].rearrange("p (k n) -> p k n", n=P),
                                oT_hi[at_].bitcast(F32), ALU.subtract).then_inc(ot_rest, 1)

            def top16(n, vals, out_v, out_i):
                for half in range(2):
                    eight = slice(8 * half, 8 * half + 8)
                    for j in range(n):
                        last = v.max(out_v[:, j, eight], vals[:, j, :])
                    step(last)
                    for j in range(n):
                        last = v.max_index(out_i[:, j, eight], out_v[:, j, eight], vals[:, j, :])
                    step(last)
                    if half == 0:
                        for j in range(n):
                            last = v.match_replace(vals[:, j, :], out_v[:, j, eight], vals[:, j, :], LOWEST)
                        step(last)

            def route(l, j, t):
                v.wait_ge(rt_moved, len(UNITS) * l + T * j + t + 1)
                top16(4, sc[:, j % 2, t, :].rearrange("p (c k) -> p c k", k=NKEYS), top, topi)
                v.tensor_copy(topf[:], topi[:])
                halves = top[:].rearrange("p (h c) k -> p h c k", c=2)
                step(v.tensor_tensor(cand[:, t].rearrange("p h (i j) -> p h i j", j=TOPK),
                                     halves[:, :, 0, :].unsqueeze(3).broadcast_to([P, 2, TOPK, TOPK]),
                                     halves[:, :, 1, :].unsqueeze(2).broadcast_to([P, 2, TOPK, TOPK]), ALU.add))
                top16(2, cand[:, t], best, pos[:, 0, :].rearrange("p (h k) -> p h k", h=2))
                at_ = slice(2 * TOPK * j, 2 * TOPK * (j + 1))
                v.tensor_tensor(gate[:, t, at_].rearrange("p (h k) -> p h k", h=2), best[:],
                                best[:, :, 0:1].broadcast_to([P, 2, TOPK]), ALU.subtract).then_inc(gate_sub, 1)
                v.tensor_scalar(pos[:, 1, :], pos[:, 0, :], 4, None, ALU.logical_shift_right)
                step(v.tensor_scalar(pos[:, 2, :], pos[:, 0, :], TOPK - 1, None, ALU.bitwise_and))
                step(v.tensor_copy(posf[:], pos[:, 1:3, :]))
                step(v.tensor_tensor(hot[:], posf[:].unsqueeze(3).broadcast_to([P, 2, 2 * TOPK, TOPK]),
                                     iota16[:].unsqueeze(1).unsqueeze(1).broadcast_to([P, 2, 2 * TOPK, TOPK]),
                                     ALU.is_equal))
                keys = topf[:].rearrange("p (h c) k -> p h c k", c=2)
                for c in range(2):
                    h4 = hot[:, c].rearrange("p (h n) k -> p h n k", h=2)
                    last = v.tensor_tensor(h4, h4, keys[:, :, c, :].unsqueeze(2).broadcast_to([P, 2, TOPK, TOPK]),
                                           ALU.mult)
                step(last)
                step(v.tensor_reduce(key[:], hot[:], AX_X, ALU.add))
                if l:
                    step(v.tensor_scalar(key[:, 1, :], key[:, 1, :], float(l * NKEYS * NKEYS), None, ALU.add))
                ins = v.scalar_tensor_tensor(out=idx[:, t, at_], in0=key[:, 0, :], scalar=float(NKEYS),
                                             in1=key[:, 1, :], op0=ALU.mult, op1=ALU.add)
                ins.then_inc(routed, 1)
                v.wait_ge(routed, len(UNITS) * l + T * j + t + 1)

            def dot_batch(t, col, batch, it=0, stride=0):
                v.wait_ge(dots_kept, it * stride + batch + 1)
                for r in range(RING):
                    v.wait_ge(rows_in[r], it * (16 * stride) + 16 * (batch + 1))
                    v.tensor_tensor_reduce(ring[:, r, :], ring[:, r, :], xt[:, t, :], 1.0, 0.0, ALU.mult, ALU.add,
                                           act8[:, r:r + 1]).then_inc(slot_free, 1)
                v.wait_ge(slot_free, it * (stride * RING) + (batch + 2) * RING)
                v.tensor_copy(act[:, t, bass.ds(it * (stride * RING) + col, RING)], act8[:]).then_inc(dots_kept, 1)

            def weigh(l, t):
                if T * l + t:
                    v.wait_ge(pickT_done, T * l + t)
                v.tensor_scalar(pick[:, 1, :], idx[:, t, :], NKEYS - 1, None, ALU.bitwise_and)
                step(v.tensor_scalar(pick[:, 0, :], idx[:, t, :], 7, None, ALU.logical_shift_right))
                step(v.tensor_scalar(pick[:, 0, :], pick[:, 0, :], NKEYS - 1, None, ALU.bitwise_and))
                step(v.tensor_copy(pickf[:], pick[:]))
                gate_h = gate[:, t, :].rearrange("p (h k) -> p h k", h=PH)
                v.wait_ge(gate_exp, T * l + t + 1)
                step(v.tensor_reduce(gsum[:, 0, :], gate_h, AX_X, ALU.add))
                step(v.reciprocal(gsum[:, 1, :], gsum[:, 0, :]))
                step(v.tensor_tensor(gate_h, gate_h, gsum[:, 1, :].unsqueeze(2).broadcast_to([P, PH, TOPK]), ALU.mult))
                v.wait_ge(gelu_done, T * l + t + 1)
                v.tensor_tensor(act[:, t, :], gate[:, t, :], act[:, t, :], ALU.mult).then_inc(picks_ready, 1)
                v.wait_ge(pickT_moved, T * l + t + 1)

            def one_hots(l, t, tok, buf, g, it, stride):
                v.wait_ge(spread_done, it * (2 * stride) + 2 * g + 2)
                for r in range(SPREAD):
                    token = bass.ds(it * (stride * SPREAD) + tok + r, 1)
                    v.tensor_scalar(onehot[:, buf, 0, r, :], iota_keys[:], pickT[:, 1, token], None, ALU.is_equal)
                    last = v.tensor_scalar(onehot[:, buf, 1, r, :], iota_keys[:], pickT[:, 0, token],
                                           pickT[:, 2, token], ALU.is_equal, ALU.mult)
                    if r % 4 == 3:
                        last.then_inc(onehot_ready, 1)

            def add_rows(l, t, col, n, it, stride):
                acc = vsum(t)
                job = l * JOBS + t * PICKS + col
                for r in range(n):
                    v.wait_ge(vrows_in[r % VRING], it * (16 * stride // VRING) + 16 * ((job + r) // VRING + 1))
                    v.scalar_tensor_tensor(out=acc, in0=vring[:, r % VRING, :],
                                           scalar=act[:, t, bass.ds(it * stride + col + r, 1)],
                                           in1=acc, op0=ALU.mult, op1=ALU.add).then_inc(vslot_free, 1)
                    v.wait_ge(vslot_free, it * stride + job + r + 1 + VRING)

            def add_half(l, t, half):
                xs = xt[:, t, half * VG:(half + 1) * VG]
                ins = v.scalar_tensor_tensor(out=xs, in0=xs, scalar=ALPHA, in1=vsum(t), op0=ALU.mult, op1=ALU.add)
                if half == 0:
                    ins.then_inc(gathered, 1)
                    v.wait_ge(gathered, T * l + t + 1)
                else:
                    step(ins)
                for c in range(2 * half, 2 * half + 2):
                    last = v.bn_stats(stats[:, t, c, :], xt[:, t, c * GROUP:(c + 1) * GROUP])
                step(last)

            v.wait_ge(small_in, 6 * 16)
            step(v.tensor_scalar(sink8[:], sink8[:], 1.0 / SCALE, None, ALU.mult))
            for j in range(2):
                v.tensor_tensor_reduce(lamv[:, 2 * j, :], lamv[:, 2 * j, :], lamv[:, 2 * j + 1, :], 1.0, 0.0, ALU.mult,
                                       ALU.add, sm[:, j:j + 1]).then_inc(lam_dot, 1)
            v.wait_ge(const_pool, 9)
            for l in range(DEPTH):
                if l == 1:
                    v.wait_ge(lam_exp, 1)
                    step(v.tensor_tensor(sm[:, 4:5], sm[:, 3:4], sm[:, 2:3], ALU.subtract))
                    step(v.tensor_scalar(sm[:, 5:6], sm[:, 4:5], -(0.8 - 0.6 * math.exp(-0.3 * l)), None, ALU.add))
                rest_xT(2 * l)
                low_part(l, 0)
                for i in range(WQ_SLOT[l]):
                    for g in finished(l, i):
                        if g >= QKV[l]:
                            residual(l, g)
                    low_part(l, i + 1)
                    s3, s1, s0 = step_at(l, i - 3), step_at(l, i - 1), step_at(l, i)
                    if s1 is not None:
                        norm(l, s1)
                    if s3 is not None:
                        move(l, s3)
                        if l == 1 and s3 % 2 == 1:
                            sub_norm(l, s3 // 2)
                    for u in unit_at(l, i):
                        unit_rest(u)
                    if s0 is not None:
                        bias(l, s0)
                residual(l, QKV[l] + 3)
                for t in range(T):
                    layer_norm(2 * T * l + t, t, gb1)
                rest_xT(2 * l + 1)
                b0 = l * BATCHES
                early = 0
                for n, (j, t) in enumerate(UNITS):
                    route(l, j, t)
                    if n >= T and n < len(UNITS) - 1:
                        je, te = DOTS[early // UB]
                        if early == 0:
                            for m in range(T):
                                ln_finished(v, 2 * T * l + m)
                        dot_batch(te, 2 * TOPK * je + (early % UB) * RING, b0 + early)
                        early += 1
                while early % UB:
                    j, t = DOTS[early // UB]
                    dot_batch(t, 2 * TOPK * j + (early % UB) * RING, b0 + early)
                    early += 1
                for n in range(early // UB, len(DOTS)):
                    j, t = DOTS[n]
                    if n == TB // UB:
                        weigh(l, 0)
                    with v.Fori(0, UB // 2) as it:
                        for half in range(2):
                            dot_batch(t, 2 * TOPK * j + half * RING, b0 + n * UB + half, it, 2)
                            if t:
                                b = (n - TB // UB) * UB + half
                                one_hots(l, 0, b * SPREAD, half, T * TB * l + b, it, 2)
                weigh(l, 1)
                step(v.memset(vsum(0), 0.0))
                with v.Fori(0, TB // 2) as it:
                    for half in range(2):
                        one_hots(l, 1, half * SPREAD, half, TB * (T * l + 1) + half, it, 2)
                        add_rows(l, 0, half * VRING, VRING, it, 2 * VRING)
                with v.Fori(0, TB // 2) as it:
                    add_rows(l, 0, PICKS // 2, RING, it, RING)
                add_half(l, 0, 0)
                v.wait_ge(spread_moved, 2 * TB * T * (l + 1) + 2)
                step(v.memset(vsum(1), 0.0))
                with v.Fori(0, TB) as it:
                    add_rows(l, 1, 0, RING, it, RING)
                add_half(l, 1, 0)
                for t in range(T):
                    v.wait_ge(vout_turned, T * l + t + 1)
                    add_half(l, t, 1)
                    layer_norm(2 * T * l + T + t, t, gb2)


_INS = ['x', 'a_w_qkv', 'a_sinks', 'a_w_o', 'b_w_qkv', 'b_lambda_q1', 'b_lambda_k1', 'b_lambda_q2', 'b_lambda_k2',
        'b_subln_g', 'b_w_o', 'ln1_g', 'ln1_b', 'ln2_g', 'ln2_b', 'peer_w_q', 'peer_subkeys', 'peer_u', 'peer_v']


def kernel(**inputs):
    import numpy as _np
    import concourse.bacc as _bacc
    from concourse import mybir as _mybir
    from concourse.bass_utils import run_bass_kernel_spmd as _run

    nc = _bacc.Bacc("TRN2", target_bir_lowering=False, num_devices=1)
    arrays, args = {}, []
    for name in _INS:
        a = _np.ascontiguousarray(inputs[name])
        arrays[f"in_{name}_dram"] = a
        args.append(nc.dram_tensor(f"in_{name}_dram", a.shape, _mybir.dt.from_np(a.dtype), kind="ExternalInput").ap())
    shape = inputs["x"].shape
    args.append(nc.dram_tensor("out_0_dram", shape, _mybir.dt.from_np(_np.dtype("float32")),
                               kind="ExternalOutput").ap())
    decoder_trunk(nc, *args)
    r = _run(nc, [arrays], core_ids=[0])
    return r.results[0]["out_0_dram"]
```

```python
import math
from contextlib import ExitStack

import numpy as np

import concourse.bass as bass
from concourse import mybir

ALU = mybir.AluOpType
ACT = mybir.ActivationFunctionType
F32 = mybir.dt.float32
F32R = mybir.dt.float32r
U32 = mybir.dt.uint32
AX_X = mybir.AxisListType.X

P = 128
LN_EPS = 1e-5
MASKED = -1e32
LOWEST = -3.0e38
RING = 8
VRING = 4


def alibi(n):
    return [float(s) for s in (2.0 ** (-8.0 * np.arange(1, n + 1) / n)).astype(np.float32)]


def decoder_trunk(nc, x, a_w_qkv, a_sinks, a_w_o, b_w_qkv, b_lambda_q1, b_lambda_k1, b_lambda_q2, b_lambda_k2,
                  b_subln_g, b_w_o, ln1_g, ln1_b, ln2_g, ln2_b, peer_w_q, peer_subkeys, peer_u, peer_v, out):
    _, SEQ, D = x.shape
    DEPTH = ln1_g.shape[0]
    A_HEADS = a_sinks.shape[1]
    HD = b_lambda_q1.shape[1]
    A_KV = (a_w_qkv.shape[2] // HD - A_HEADS) // 2
    VD = b_subln_g.shape[1]
    B_HEADS = b_w_o.shape[1] // VD
    PH, NKEYS, PHALF = peer_subkeys.shape[1], peer_subkeys.shape[3], peer_subkeys.shape[4]
    HC = 2 * PH
    TOPK = 16
    PICKS = PH * TOPK
    T = SEQ // P
    KT = D // P
    ALPHA = (2.0 * DEPTH) ** 0.25
    SCALE = HD ** -0.5
    GROUP = 512
    KK = 4
    CH = KT // KK
    BPG = GROUP // P
    POOL_KK = 3
    POOL_FROM = 1344
    assert T == 2 and D == 2048 and HD == 64 and PICKS == P and NKEYS == P and PHALF == P and DEPTH == 2
    slopes = [alibi(A_HEADS), alibi(B_HEADS)]

    LATE_PAIR = [(0, 0), (0, 1), (0, 2), (1, 0), (1, 1), (1, 2), (0, 3), (1, 3), (2, 0), (2, 1), (2, 2), (2, 3),
                 (3, 0), (3, 1), (3, 2), (3, 3)]

    def stream(l):
        if l == 0:
            cols = [A_HEADS * HD] + [g * GROUP for g in range(4)]
        else:
            cols = [c * D + h * GROUP for h in range(4) for c in range(3)]
        out = [("qkv", col, q, g) for g, col in enumerate(cols) for q in range(CH)]
        n = len(cols)
        out += [("wo", g * GROUP, q, n + g) for g, q in LATE_PAIR]
        out += [("wq", g * GROUP, q, n + 4 + g) for g in range(4) for q in range(CH)]
        return out

    STREAM = [stream(l) for l in range(DEPTH)]
    C0 = [0, len(STREAM[0])]
    G0 = [0, len(STREAM[0]) // CH]
    NCHUNKS = sum(len(s) for s in STREAM)
    QKV = [5, 12]
    JOBS = T * PICKS
    BATCHES = JOBS // RING
    TB = BATCHES // T
    VG = D // 2
    VB = (D - VG) // P
    SPREAD = 8
    assert P // SPREAD == TB
    STEPS = 16
    WQ_SLOT = [CH * (QKV[l] + 4) for l in range(DEPTH)]

    EARLY_FROM, EARLY = [s + 6 for s in WQ_SLOT], 3

    def last_chunk(l, g):
        return max(i for i, c in enumerate(STREAM[l]) if c[3] == g)

    def group_done(l, g):
        return C0[l] + last_chunk(l, g) + 1

    def dve_shares(l, i):
        return i < WQ_SLOT[l] + CH

    def dve_lows(c):
        return sum(dve_shares(l, i) for l in range(DEPTH) for i in range(len(STREAM[l])) if C0[l] + i < c)

    def finished(l, i):
        return [g for g in range(len(STREAM[l]) // CH) if last_chunk(l, g) == i - 1]

    def place(l, s):
        return (s % 2, s // 2) if l == 0 else ((s % 4) // 2, 2 * (s // 4) + s % 2)

    def slot_of(l, s):
        if l == 0:
            return 8 + s
        return 12 * (s // 4 + 1) + 2 * (s % 4) if s // 4 < 3 else 12 * 4 - 3 + s % 4

    def step_at(l, i):
        found = [s for s in range(STEPS) if slot_of(l, s) == i]
        return found[0] if found else None

    def unit_at(l, i):
        if l == 0:
            return []
        return [2 * h + t for h in range(4) for t in range(T) if 12 * (h + 1) + (10 if h < 3 else 4) + t == i]

    def blocks_before(s):
        return sum(place(0, j)[0] + 1 for j in range(s))

    def turned(l, s):
        return blocks_before(s + 1) if l == 0 else blocks_before(STEPS) + s + 1

    with ExitStack() as ctx:
        def sem(name):
            return ctx.enter_context(nc.semaphore(name))

        base = -(-nc.sbuf_base // 64) * 64
        top_of = [0]

        def at(name, offset, shape, dt=F32):
            size = int(np.prod(shape[1:])) * 4
            top_of[0] = max(top_of[0], offset + size)
            return nc.alloc_sbuf_tensor_at(name, shape, dt, offset=base + offset)

        K = 1024
        xt = at("xt", 0, [P, T, D])
        raw = at("raw", 16 * K, [P, 2, KK, GROUP])
        w_hi = at("w_hi", 32 * K, [P, 2, KK, GROUP], F32R)
        w_lo = at("w_lo", 48 * K, [P, 2, KK, GROUP], F32R)
        xT_hi = at("xT_hi", 64 * K, [P, KT, T * P], F32R)
        xT_lo = at("xT_lo", 80 * K, [P, KT, T * P], F32R)
        oT_hi = at("oT_hi", 96 * K, [P, KT, T * P], F32R)
        oT_lo = at("oT_lo", 112 * K, [P, KT, T * P], F32R)
        qT = at("qT", 128 * K, [P, 2, BPG, T * P])
        kT = at("kT", 136 * K, [P, 2, BPG, T * P])
        vn = at("vn", 144 * K, [P, 2, T, GROUP])
        prob = at("prob", 152 * K, [P, 3, 4, 2 * P])
        pT = at("pT", 164 * K, [P, 2, 2, GROUP])
        orow = at("orow", 172 * K, [P, 2, GROUP])
        osq = at("osq", 176 * K, [P, GROUP])
        gb1 = at("gb1", 178 * K, [P, 2, D])
        skn = at("skn", 128 * K, [P, HC, PHALF])
        ring = at("ring", 96 * K, [P, RING, D])
        skT = at("skT", 160 * K, [P, HC, NKEYS])
        pqT = at("pqT", 168 * K, [P, 2, BPG, T * P])
        sc = at("sc", 176 * K, [P, PH // 2, T, 4 * NKEYS])
        hot = at("hot", 192 * K, [P, 2 * TOPK, TOPK])
        spread = at("spread", 16 * K, [P, T, NKEYS, P])
        onehot = at("onehot", 160 * K, [P, 2, 2, SPREAD, P])
        vring = at("vring", 176 * K, [P, VRING, VG])
        vblk = at("vblk", 144 * K, [P, VRING, D - VG])
        pick = at("pick", 192 * K, [P, 2, PICKS], U32)
        pickf = at("pickf", 193 * K, [P, 2, PICKS])
        gb2 = at("gb2", 160 * K, [P, 2, D])
        vout = at("vout", 64 * K, [P, VB, T * P])
        small_at = [194 * K]

        def small(name, shape, dt=F32):
            t = at(name, small_at[0], shape, dt)
            small_at[0] += -(-int(np.prod(shape[1:])) * 4 // 32) * 32
            return t

        ident = small("ident", [P, P])
        mask = small("mask", [P, 2, 2 * P])
        cand = small("cand", [P, 2, TOPK * TOPK])
        iota16 = small("iota16", [P, TOPK])
        iota_keys = small("iota_keys", [P, NKEYS])
        one = small("one", [P, 1])
        pickT = small("pickT", [P, 3, P])
        sink8 = small("sink8", [P, A_HEADS])
        lamv = small("lamv", [P, 4, HD])
        subg = small("subg", [P, VD])
        sm = small("sm", [P, 8])
        mx = small("mx", [P, 2, 4])
        nm = small("nm", [P, 2, 4])
        rs = small("rs", [P, 2, 4])
        sk = small("sk", [P, 2, 4])
        rd = small("rd", [P, 2, 4])
        sq = small("sq", [P, 3, 4])
        stats = small("stats", [P, T, 4, 6])
        mv = small("mv", [P, T, 5])
        top = small("top", [P, 4, TOPK])
        topi = small("topi", [P, 4, TOPK], U32)
        topf = small("topf", [P, 4, TOPK])
        best = small("best", [P, 2, TOPK])
        pos = small("pos", [P, 3, 2 * TOPK], U32)
        posf = small("posf", [P, 2, 2 * TOPK])
        key = small("key", [P, 2, 2 * TOPK])
        gsum = small("gsum", [P, 2, PH])
        idx = small("idx", [P, T, PICKS], U32)
        idxs = small("idxs", [P, 2, RING], U32)
        gate = small("gate", [P, T, PICKS])
        act8 = small("act8", [P, RING])
        act = small("act", [P, T, PICKS])
        assert base + top_of[0] <= nc.sbuf_usable_end, (base, top_of[0], nc.sbuf_usable_end)
        ps = ctx.enter_context(nc.psum_tensor("ps", [P, 8, 512], F32))

        x_in = [sem(f"x_in{t}") for t in range(T)]
        small_in = sem("small_in")
        gb_in = sem("gb_in")
        sk_in = sem("sk_in")
        w_in = [sem(f"w_in{r}") for r in range(2)]
        hi_done = sem("hi_done")
        lo_pool = sem("lo_pool")
        lo_dve = sem("lo_dve")
        w_used = sem("w_used")
        rows_in = [sem(f"rows_in{r}") for r in range(RING)]
        slot_free = sem("slot_free")
        idx_staged = sem("idx_staged")
        gathers_begun = sem("gathers_begun")
        out_done = sem("out_done")
        const_pool = sem("const_pool")
        xT_done = sem("xT_done")
        xT_top = sem("xT_top")
        xT_rest = sem("xT_rest")
        proj_free = sem("proj_free")
        k_spread = sem("k_spread")
        sc_done = sem("sc_done")
        sc_ready = sem("sc_ready")
        sc_exp = sem("sc_exp")
        prob_ready = sem("prob_ready")
        pt_done = sem("pt_done")
        pt_moved = sem("pt_moved")
        pv_done = sem("pv_done")
        pv_top = sem("pv_top")
        pv_moved = sem("pv_moved")
        sub_sq = sem("sub_sq")
        sub_rt = sem("sub_rt")
        sub_done = sem("sub_done")
        ot_done = sem("ot_done")
        ot_top = sem("ot_top")
        ot_rest = sem("ot_rest")
        lam_dot = sem("lam_dot")
        lam_exp = sem("lam_exp")
        ln_var = sem("ln_var")
        ln_root = sem("ln_root")
        ln_recip = sem("ln_recip")
        ln_scaled = sem("ln_scaled")
        ln_done = sem("ln_done")
        ln_pool = sem("ln_pool")
        pool_step = sem("pool_step")
        skT_done = sem("skT_done")
        skT_moved = sem("skT_moved")
        rt_done = sem("rt_done")
        rt_moved = sem("rt_moved")
        gate_sub = sem("gate_sub")
        gate_exp = sem("gate_exp")
        routed = sem("routed")
        vrows_in = [sem(f"vrows_in{r}") for r in range(VRING)]
        vslot_free = sem("vslot_free")
        vrow_begun = sem("vrow_begun")
        vblk_in = [sem(f"vblk_in{r}") for r in range(VRING)]
        vblk_used = sem("vblk_used")
        picks_ready = sem("picks_ready")
        pickT_done = sem("pickT_done")
        pickT_moved = sem("pickT_moved")
        apart_ready = sem("apart_ready")
        apart_abs = sem("apart_abs")
        hot2_ready = sem("hot2_ready")
        hot1_ready = sem("hot1_ready")
        hot1_weighed = sem("hot1_weighed")
        spread_done = sem("spread_done")
        spread_moved = sem("spread_moved")
        gathered = sem("gathered")
        vout_moved = sem("vout_moved")
        vout_turned = sem("vout_turned")
        dots_kept = sem("dots_kept")
        gelu_done = sem("gelu_done")
        dve_step = sem("dve_step")

        W = {("qkv", 0): a_w_qkv[0], ("qkv", 1): b_w_qkv[0], ("wo", 0): a_w_o[0], ("wo", 1): b_w_o[0]}
        W.update({("wq", l): peer_w_q[l] for l in range(DEPTH)})

        def ln_finished(eng, n):
            eng.wait_ge(ln_done, n + 1)
            eng.wait_ge(ln_pool, n + 1)

        UNITS = [(j, t) for t in range(T) for j in range(PH // 2)]
        UB = 2 * TOPK // RING
        ROUTES = len(UNITS) + 1

        def x_bank(n, t):
            return 4 * (t if n % 2 == 0 else 1 - t)

        def gain_shift(eng, dst, g, b, l):
            for j, v in enumerate((g, b)):
                eng.dma_start(dst[:, j, :], v[l:l + 1, :].broadcast_to([P, D])).then_inc(gb_in, 16)

        def vsum(t):
            lo = 6 - 2 * t
            return ps[:, lo:lo + 2, :].rearrange("p b n -> p (b n)")

        block = ctx.enter_context(nc.Block())

        @block.sync
        def _(sp):
            for t in range(T):
                sp.dma_start(xt[:, t, :], x[0, t * P:(t + 1) * P, :]).then_inc(x_in[t], 16)

            for l in range(DEPTH):
                for i, (name, col, q, _g) in enumerate(STREAM[l]):
                    c = C0[l] + i
                    if c >= 2:
                        sp.wait_ge(hi_done, c - 1)
                        sp.wait_ge(lo_pool, c - 1)
                        if dve_lows(c - 1) > dve_lows(c - 2):
                            sp.wait_ge(lo_dve, dve_lows(c - 1))
                    src = W[name, l].rearrange("(q k p) n -> q p k n", p=P, k=KK)[q][:, :, col:col + GROUP]
                    sp.dma_start(raw[:, c % 2], src).then_inc(w_in[c % 2], 16)
                    if i == 8:
                        if l:
                            ln_finished(sp, 2 * T * l - 1)
                        gain_shift(sp, gb1, ln1_g, ln1_b, l)
                    if i == WQ_SLOT[l] - 7:
                        sp.wait_ge(pv_moved, STEPS * (l + 1))
                        sp.dma_start(skn[:], peer_subkeys[l].rearrange("h c k d -> k (h c) d")).then_inc(sk_in, 16)
                sp.wait_ge(slot_free, RING + JOBS * (l + 1))
                experts = peer_v.rearrange("l e d -> (l e) d")
                with sp.Fori(0, NKEYS // VRING) as it:
                    for r in range(VRING):
                        sp.wait_ge(vblk_used, it * VRING + l * NKEYS + r + 1)
                        sp.dma_start(vblk[:, r, :], experts[bass.ds(it * (VRING * P) + (l * NKEYS + r) * P, P), VG:D]
                                     ).then_inc(vblk_in[r], 16)
                sp.wait_ge(vblk_used, NKEYS * (l + 1) + VRING)
                sp.wait_ge(gathered, T * (l + 1))
            for t in range(T):
                ln_finished(sp, 2 * T * (DEPTH - 1) + T + t)
                sp.dma_start(out[0, t * P:(t + 1) * P, :], xt[:, t, :]).then_inc(out_done, 16)
            sp.wait_ge(out_done, 16 * T)

        @block.gpsimd
        def _(pool):
            pool.memset(ident[:], 0.0).then_inc(const_pool, 1)
            for m in range(2):
                pool.iota(mask[:, m, :], [[1, 2 * P]], base=-P, channel_multiplier=-1,
                          allow_small_or_imprecise_dtypes=True).then_inc(const_pool, 1)
            pool.iota(iota16[:], [[1, TOPK]], base=0, channel_multiplier=0,
                      allow_small_or_imprecise_dtypes=True).then_inc(const_pool, 1)
            pool.iota(iota_keys[:], [[1, NKEYS]], base=0, channel_multiplier=0,
                      allow_small_or_imprecise_dtypes=True).then_inc(const_pool, 1)
            pool.memset(one[:], 1.0).then_inc(const_pool, 1)
            pool.wait_ge(const_pool, 6)
            pool.affine_select(out=ident[:], in_=ident[:], compare_op=ALU.not_equal, fill=1.0, base=0,
                               pattern=[[-1, P]], channel_multiplier=1).then_inc(const_pool, 1)
            for m in range(2):
                pool.affine_select(out=mask[:, m, :], in_=mask[:, m, :], compare_op=ALU.is_ge, fill=MASKED, base=P,
                                   pattern=[[-1, 2 * P]], channel_multiplier=1).then_inc(const_pool, 1)
            pool.wait_ge(const_pool, 9)
            pool.affine_select(out=mask[:, 0, :], in_=mask[:, 0, :], compare_op=ALU.is_ge, fill=MASKED, base=-1,
                               pattern=[[1, 2 * P]], channel_multiplier=-1).then_inc(const_pool, 1)
            steps = [0]

            def low_part(l, i):
                c = C0[l] + i
                share = POOL_KK if dve_shares(l, i) else KK
                pool.wait_ge(hi_done, c + 1)
                if c >= 2:
                    pool.wait_ge(w_used, c - 1)
                r = c % 2
                pool.tensor_tensor(w_lo[:, r, 0:share, :], raw[:, r, 0:share, :],
                                   w_hi[:, r, 0:share, :].bitcast(F32), ALU.subtract).then_inc(lo_pool, 1)

            def norm_share(n, t, gb):
                pool.wait_ge(ln_scaled, n + 1)
                pool.wait_ge(gb_in, 32 * (n // T + 1))
                xs = xt[:, t, POOL_FROM:D]
                pool.tensor_tensor(xs, xs, gb[:, 0, POOL_FROM:D], ALU.mult).then_inc(pool_step, 1)
                steps[0] += 1
                pool.wait_ge(pool_step, steps[0])
                pool.tensor_tensor(xs, xs, gb[:, 1, POOL_FROM:D], ALU.add).then_inc(ln_pool, 1)

            def gather_u(t, col, batch, half, it=0, stride=0, rows=range(RING)):
                if rows[0] == 0:
                    stage_u(t, col, batch, half, it, stride)
                for r in rows:
                    pool.wait_ge(slot_free, it * (stride * RING) + batch * RING + r + 1)
                    pool.sem_inc(gathers_begun, 1)
                    pool.indirect_dma_start(
                        out=ring[:, r, :], out_offset=None, in_=peer_u.rearrange("l e d -> (l e) d"),
                        in_offset=bass.IndirectOffsetOnAxis(ap=idxs[:, half, r:r + 1], axis=0),
                    ).then_inc(rows_in[r], 16)

            def stage_u(t, col, batch, half, it, stride):
                pool.tensor_copy(idxs[:, half, :], idx[:, t, bass.ds(it * (stride * RING) + col, RING)]
                                 ).then_inc(idx_staged, 1)
                pool.wait_ge(idx_staged, it * stride + batch // BATCHES * BATCHES + batch + 1)

            def key_distances(tok, buf, g, it, stride):
                pool.wait_ge(spread_done, it * (2 * stride) + 2 * g + 2)
                keys = pickT[:, 1, bass.ds(it * (stride * SPREAD) + tok, SPREAD)]
                pool.tensor_tensor(onehot[:, buf, 0], keys.unsqueeze(2).broadcast_to([P, SPREAD, P]),
                                   iota_keys[:].unsqueeze(1).broadcast_to([P, SPREAD, P]), ALU.subtract
                                   ).then_inc(apart_ready, 1)

            def gather_v(l, t, half, it, spreads=False):
                picks = idx[:, t, bass.ds(it * (2 * RING) + half * RING, RING)]
                pool.tensor_tensor(idxs[:, half, :], picks, picks, ALU.add).then_inc(idx_staged, 1)
                pool.wait_ge(idx_staged, it * 2 + (2 * l + 1) * BATCHES + t * TB + half + 1)
                for r in range(RING):
                    pool.wait_ge(vslot_free, it * (2 * RING) + l * JOBS + t * PICKS + half * RING + r + 1)
                    pool.sem_inc(gathers_begun, 1)
                    pool.indirect_dma_start(
                        out=vring[:, r % VRING, :], out_offset=None,
                        in_=peer_v.rearrange("l e (h d) -> (l e h) d", d=VG),
                        in_offset=bass.IndirectOffsetOnAxis(ap=idxs[:, half, r:r + 1], axis=0),
                    ).then_inc(vrows_in[r % VRING], 16)
                    if spreads and r % VRING == VRING - 1:
                        b = 2 * half + r // VRING
                        pool.wait_ge(pickT_moved, T * l + 2)
                        key_distances(b * SPREAD, r // VRING, TB * (T * l + 1) + b, it, 4)

            for l in range(DEPTH):
                b0 = l * BATCHES

                def unit_routed(n):
                    pool.wait_ge(routed, ROUTES * l + n + 2)

                def early(rows):
                    for row in rows:
                        b, r = divmod(row, RING)
                        gather_u(0, b * RING, b0 + b, b % 2, rows=range(r, r + 1))

                for i in range(1 if l else 0, len(STREAM[l])):
                    low_part(l, i)
                    if i == WQ_SLOT[l]:
                        for t in range(T):
                            norm_share(2 * T * l + t, t, gb1)
                    n = i - EARLY_FROM[l]
                    if n == 0:
                        pool.wait_ge(routed, ROUTES * l + 1)
                    elif n == TOPK // EARLY:
                        unit_routed(0)
                    if n >= 0:
                        early(range(EARLY * n, EARLY * (n + 1)))
                early(range(EARLY * (len(STREAM[l]) - EARLY_FROM[l]), UB * RING))
                for n, (j, t) in enumerate(UNITS[1:], 1):
                    unit_routed(n)
                    with pool.Fori(0, UB // 2) as it:
                        for half in range(2):
                            gather_u(t, 2 * TOPK * j + half * RING, b0 + n * UB + half, half, it, 2)
                            if t:
                                b = j * UB + half
                                if j == 0 and half == 0:
                                    pool.wait_ge(pickT_moved, T * l + 1)
                                key_distances(b * SPREAD, half, T * TB * l + b, it, 2)
                with pool.Fori(0, TB // 4) as it:
                    for half in range(2):
                        gather_v(l, 0, half, it, spreads=True)
                with pool.Fori(TB // 4, TB // 2) as it:
                    for half in range(2):
                        gather_v(l, 0, half, it)
                with pool.Fori(0, TB // 2) as it:
                    for half in range(2):
                        gather_v(l, 1, half, it)
                for t in range(T):
                    norm_share(2 * T * l + T + t, t, gb2)
                if l + 1 < DEPTH:
                    low_part(l + 1, 0)

        @block.scalar
        def _(a):
            a.dma_start(sink8[:], a_sinks[0:1, :].broadcast_to([P, A_HEADS])).then_inc(small_in, 16)
            for j, v in enumerate((b_lambda_q1, b_lambda_k1, b_lambda_q2, b_lambda_k2)):
                a.dma_start(lamv[:, j, :], v[0:1, :].broadcast_to([P, HD])).then_inc(small_in, 16)
            a.dma_start(subg[:], b_subln_g[0:1, :].broadcast_to([P, VD])).then_inc(small_in, 16)

            def high_part(c):
                a.wait_ge(w_in[c % 2], 16 * (c // 2 + 1))
                if c >= 2:
                    a.wait_ge(w_used, c - 1)
                a.copy(w_hi[:, c % 2], raw[:, c % 2]).then_inc(hi_done, 1)

            def top_xT(n):
                for t in range(T):
                    for b in range(4):
                        a.wait_ge(xT_done, (n * T + t) * 4 + b + 1)
                        a.copy(xT_hi[:, 4 * b:4 * b + 4, t * P:(t + 1) * P],
                               ps[:, x_bank(n, t) + b, :].rearrange("p (k n) -> p k n", n=P)).then_inc(xT_top, 1)

            def root(n):
                a.wait_ge(ln_var, n + 1)
                a.activation(mv[:, n % T, 2:3], mv[:, n % T, 1:2], ACT.Sqrt).then_inc(ln_root, 1)

            def centre(n):
                t = n % T
                a.wait_ge(ln_recip, n + 1)
                xs = xt[:, t, POOL_FROM:D]
                a.activation(xs, xs, ACT.Identity, bias=mv[:, t, 4:5], scale=mv[:, t, 3:4]
                             ).then_inc(ln_scaled, 1)

            def move_group(l, g):
                if QKV[l] <= g < QKV[l] + 4:
                    return
                G = G0[l] + g
                lo = 2 * (G % 2)
                a.wait_ge(w_used, group_done(l, g))
                if g >= QKV[l] + 4:
                    j = g - QKV[l] - 4
                    if j >= 2:
                        a.wait_ge(rt_done, len(UNITS) * l + T * (j - 1))
                    dst = pqT[:, j % 2]
                elif l == 0 and g == 0:
                    a.copy(kT[:, 1, 0:2, :], ps[:, 0, :].rearrange("p (k n) -> p k n", n=T * P))
                    a.copy(vn[:, 0, :, 0:A_KV * HD], ps[:, 1, :].rearrange("p (t n) -> p t n", t=T)
                           ).then_inc(proj_free, 1)
                    a.wait_ge(proj_free, 1)
                    for src in range(2):
                        for dst in range(2):
                            a.dma_start(kT[HD * dst:HD * (dst + 1), 0, src::2, :],
                                        kT[HD * src:HD * (src + 1), 1, 0:2, :]).then_inc(k_spread, 16)
                    return
                elif l == 0:
                    if g - 1 >= 2:
                        a.wait_ge(sc_done, 4 * (g - 2))
                    dst = qT[:, (g - 1) % 2]
                else:
                    h = g // 3
                    if h >= 2:
                        a.wait_ge(pv_done, STEPS + 4 * (h - 1))
                    if g % 3 == 2:
                        for t in range(T):
                            last = a.copy(vn[:, h % 2, t, :], ps[:, lo + t, :])
                        last.then_inc(proj_free, 1)
                        return
                    dst = (qT if g % 3 == 0 else kT)[:, h % 2]
                for b in range(2):
                    last = a.copy(dst[:, 2 * b:2 * b + 2, :], ps[:, lo + b, :].rearrange("p (k n) -> p k n", n=T * P))
                last.then_inc(proj_free, 1)

            def exps(l, s):
                t, _ = place(l, s)
                w = P * (t + 1)
                a.wait_ge(sc_ready, l * STEPS + s + 1)
                for m in range(4):
                    last = a.activation(prob[:, s % 3, m, 0:w], prob[:, s % 3, m, 0:w], ACT.Exp,
                                        bias=nm[:, s % 2, m:m + 1], scale=SCALE, accum_out=rs[:, s % 2, m:m + 1])
                if l == 0:
                    last = a.activation(sk[:, s % 2, :], sk[:, s % 2, :], ACT.Exp)
                last.then_inc(sc_exp, 1)

            def move_turned(l, s, b):
                t, _ = place(l, s)
                n = turned(l, s) - (t - b if l == 0 else 0)
                a.wait_ge(pt_done, n)
                if s >= 2 and b == 0:
                    a.wait_ge(pv_done, l * STEPS + s - 1)
                if l == 0:
                    a.copy(pT[:, s % 2, b, :], ps[:, 6, :]).then_inc(pt_moved, 1)
                else:
                    a.copy(pT[:, s % 2, 0, 0:2 * P * (t + 1)], ps[:, 6, 0:2 * P * (t + 1)]).then_inc(pt_moved, 1)

            def unit(u):
                h, t = u // T, u % T
                a.wait_ge(ot_done, u + 1)
                a.copy(oT_hi[:, 4 * h:4 * h + 4, t * P:(t + 1) * P], ps[:, 7, :].rearrange("p (k n) -> p k n", n=P)
                       ).then_inc(ot_top, 1)

            def unit_root(u):
                a.wait_ge(sub_sq, u + 1)
                a.activation(sq[:, 1, :], sq[:, 0, :], ACT.Sqrt).then_inc(sub_rt, 1)

            def route_scores(l, j):
                for t in range(T):
                    a.wait_ge(rt_done, len(UNITS) * l + T * j + t + 1)
                    a.copy(sc[:, j, t, :], ps[:, 4 + 2 * (j % 2) + t, :]).then_inc(rt_moved, 1)

            def gates(l, t):
                a.wait_ge(gate_sub, ROUTES * l + PH // 2 * (t + 1) + 1)
                a.activation(gate[:, t, :], gate[:, t, :], ACT.Exp).then_inc(gate_exp, 1)

            def move_spread(l, t):
                a.wait_ge(pickT_done, T * l + t + 1)
                a.copy(pickT[:], ps[:, 4, 0:3 * P].rearrange("p (k n) -> p k n", n=P)).then_inc(pickT_moved, 1)
                g0 = TB * (T * l + t)

                def weigh_hot(buf, b, it):
                    a.wait_ge(apart_ready, it * 2 + g0 + b + 1)
                    a.activation(onehot[:, buf, 0], onehot[:, buf, 0], ACT.Abs).then_inc(apart_abs, 1)
                    a.wait_ge(hot1_ready, it * 2 + g0 + b + 1)
                    for r in range(SPREAD):
                        rows = onehot[:, buf, 1, r, :]
                        last = a.mul(rows, rows, pickT[:, 2, bass.ds(it * (2 * SPREAD) + b * SPREAD + r, 1)])
                        if r % 4 == 3:
                            last.then_inc(hot1_weighed, 1)
                    a.wait_ge(apart_abs, it * 2 + g0 + b + 1)
                    a.activation(onehot[:, buf, 0], onehot[:, buf, 0], ACT.Relu, bias=one[:], scale=-1.0
                                 ).then_inc(hot2_ready, 1)

                def move_batch(b, it):
                    for half in range(2):
                        a.wait_ge(spread_done, it * 4 + 2 * (g0 + b) + half + 1 + 4)
                        a.copy(spread[:, t, :, bass.ds(it * (2 * SPREAD) + b * SPREAD + 4 * half, 4)],
                               ps[:, 4 + half, :].rearrange("p (q k) -> p k q", q=4)).then_inc(spread_moved, 1)

                weigh_hot(0, 0, 0)
                with a.Fori(0, TB // 2 - 1) as it:
                    weigh_hot(1, 1, it)
                    move_batch(0, it)
                    weigh_hot(0, 2, it)
                    move_batch(1, it)
                if t == 0:
                    gates(l, 1)
                weigh_hot(1, TB - 1, 0)
                move_batch(TB - 2, 0)
                move_batch(TB - 1, 0)

            a.sem_inc(spread_moved, 2)
            high_part(0)
            for l in range(DEPTH):
                if l == 1:
                    a.wait_ge(lam_dot, 2)
                    a.activation(sm[:, 2:4], sm[:, 0:2], ACT.Exp).then_inc(lam_exp, 1)
                top_xT(2 * l)
                for i in range(len(STREAM[l])):
                    if i == WQ_SLOT[l]:
                        for b in range(4):
                            a.wait_ge(skT_done, l * 4 + b + 1)
                            a.copy(skT[:, 4 * b:4 * b + 4, :], ps[:, 4 + b, :].rearrange("p (k n) -> p k n", n=P)
                                   ).then_inc(skT_moved, 1)
                        for t in range(T):
                            root(2 * T * l + t)
                        for t in range(T):
                            centre(2 * T * l + t)
                        top_xT(2 * l + 1)
                    for g in finished(l, i):
                        move_group(l, g)
                    if i + 1 < len(STREAM[l]):
                        high_part(C0[l] + i + 1)
                    s3, s2, s0 = step_at(l, i - 3), step_at(l, i - 2), step_at(l, i)
                    if s3 is not None and l == 0:
                        t, hg = place(l, s3)
                        a.wait_ge(pv_done, s3 + 1)
                        a.copy(oT_hi[:, 2 * hg:2 * hg + 2, t * P:(t + 1) * P],
                               ps[:, 7, 0:2 * P].rearrange("p (j q) -> p j q", q=P)).then_inc(pv_top, 1)
                    if s3 is not None and l == 1 and s3 % 2 == 1:
                        unit_root(s3 // 2)
                    for u in unit_at(l, i):
                        unit(u)
                    if s2 is not None:
                        for b in range(place(l, s2)[0] + 1 if l == 0 else 1):
                            move_turned(l, s2, b)
                    if s0 is not None:
                        exps(l, s0)
                    j = i - WQ_SLOT[l]
                    if j > 0 and j % CH == 0:
                        route_scores(l, j // CH - 1)
                for g in finished(l, len(STREAM[l])):
                    move_group(l, g)
                route_scores(l, PH // 2 - 1)
                gates(l, 0)
                for t in range(T):
                    a.wait_ge(dots_kept, l * BATCHES + (t + 1) * TB + 1)
                    a.activation(act[:, t, :], act[:, t, :], ACT.Gelu).then_inc(gelu_done, 1)
                    move_spread(l, t)
                a.wait_ge(spread_done, 2 * T * TB * (l + 1) + 4)
                gain_shift(a, gb2, ln2_g, ln2_b, l)
                a.wait_ge(vblk_used, NKEYS * (l + 1) + VRING)
                for b in range(4):
                    a.copy(vout[:, 2 * b:2 * b + 2, :], ps[:, b, :].rearrange("p (k n) -> p k n", n=T * P)
                           ).then_inc(vout_moved, 1)
                for t in range(T):
                    root(2 * T * l + T + t)
                for t in range(T):
                    centre(2 * T * l + T + t)
                if l + 1 < DEPTH:
                    high_part(C0[l + 1])

        @block.tensor
        def _(pe):
            def transpose_x(n):
                for t in range(T):
                    if n == 0:
                        pe.wait_ge(x_in[t], 16)
                        pe.wait_ge(const_pool, 7)
                    else:
                        ln_finished(pe, T * (n - 1) + t)
                    for k in range(KT):
                        b = x_bank(n, t) + k // 4
                        last = pe.transpose(ps[:, b, (k % 4) * P:(k % 4 + 1) * P], xt[:, t, k * P:(k + 1) * P],
                                            ident[:])
                        if k % 4 == 3:
                            last.then_inc(xT_done, 1)
                pe.wait_ge(xT_top, (n + 1) * 4 * T)
                pe.wait_ge(xT_rest, (n + 1) * 4 * T)

            def subkeys(l):
                pe.wait_ge(sk_in, 16 * (l + 1))
                for k in range(HC):
                    last = pe.transpose(ps[:, 4 + k // 4, (k % 4) * P:(k % 4 + 1) * P], skn[:, k, :], ident[:])
                    if k % 4 == 3:
                        last.then_inc(skT_done, 1)
                pe.wait_ge(skT_moved, 4 * (l + 1))

            def product(out_ap, stationary, moving, start, stop):
                (s_hi, s_lo), (m_hi, m_lo) = stationary, moving
                pe.matmul(out_ap, s_hi, m_hi, start=start, stop=False, skip_group_check=True)
                pe.matmul(out_ap, s_hi, m_lo, start=False, stop=False, skip_group_check=True)
                return pe.matmul(out_ap, s_lo, m_hi, start=False, stop=stop, skip_group_check=True)

            def half_chunk(l, i, half):
                name, _col, q, g = STREAM[l][i]
                c, G = C0[l] + i, G0[l] + g
                r = c % 2
                if half == 0:
                    if q == 0 and G >= 2:
                        pe.wait_ge(proj_free, G - 1)
                    pe.wait_ge(hi_done, c + 1)
                    pe.wait_ge(lo_pool, c + 1)
                    if dve_lows(c + 1) > dve_lows(c):
                        pe.wait_ge(lo_dve, dve_lows(c + 1))
                act_hi, act_lo = (oT_hi, oT_lo) if name == "wo" else (xT_hi, xT_lo)
                by_rows = name == "wo" or (name == "qkv" and l == 1 and g % 3 == 2)
                lo = 2 * (G % 2)
                for kk in range(2 * half, 2 * half + 2):
                    k = q * KK + kk
                    stop = k == KT - 1
                    moving = (act_hi[:, k, :], act_lo[:, k, :])

                    def rows_of(t):
                        return tuple(x_[:, k, t * P:(t + 1) * P] for x_ in (act_hi, act_lo))

                    def cols(c0, n):
                        return tuple(w[:, r, kk, c0:c0 + n] for w in (w_hi, w_lo))

                    if name == "qkv" and l == 0 and g == 0:
                        for b in range(2):
                            product(ps[:, 0, b * 256:(b + 1) * 256], cols(b * P, P), moving, k == 0 and b == 0, stop)
                        for t in range(T):
                            last = product(ps[:, 1, t * 256:(t + 1) * 256], rows_of(t), cols(A_KV * HD, A_KV * HD),
                                           k == 0 and t == 0, stop)
                    elif by_rows:
                        for t in range(T):
                            last = product(ps[:, lo + t, :], rows_of(t), cols(0, GROUP), k == 0, stop)
                    else:
                        for b in range(BPG):
                            last = product(ps[:, lo + b // 2, (b % 2) * 256:(b % 2) * 256 + 256], cols(b * P, P),
                                           moving, k == 0 and b % 2 == 0, stop)
                if half:
                    last.then_inc(w_used, 1)

            def scores(l, s):
                n = l * STEPS + s
                t, hg = place(l, s)
                w = P * (t + 1)
                buf = (s // 4) % 2
                pe.wait_ge(proj_free, G0[l] + (s // 4 + 2 if l == 0 else 3 * (s // 4) + 2))
                if l == 0:
                    pe.wait_ge(k_spread, 64)
                if n:
                    pe.wait_ge(sc_ready, n)
                for m in range(4):
                    half = slice(HD * (m % 2), HD * (m % 2) + HD)
                    blk = 2 * (hg % 2) + m // 2
                    keys = kT[half, 0, hg // 2, 0:w] if l == 0 else kT[half, buf, blk, 0:w]
                    last = pe.matmul(ps[:, 4 + m % 2, (m // 2) * 256:(m // 2) * 256 + w],
                                     qT[half, buf, blk, t * P:(t + 1) * P], keys, start=True, stop=True)
                last.then_inc(sc_done, 1)

            def turn(l, s, b):
                t, _ = place(l, s)
                done = turned(l, s) - (t - b if l == 0 else 0)
                pe.wait_ge(prob_ready, l * STEPS + s + 1)
                if done > 1:
                    pe.wait_ge(pt_moved, done - 1)
                if l == 0:
                    pairs = [(j, m, b) for j, m in enumerate((0, 2, 1, 3))]
                else:
                    pairs = [(2 * bb + j, 2 * j, bb) for bb in range(t + 1) for j in range(2)]
                for col, m, bb in pairs:
                    last = pe.transpose(ps[:, 6, col * P:(col + 1) * P], prob[:, s % 3, m, bb * P:(bb + 1) * P],
                                        ident[:])
                last.then_inc(pt_done, 1)

            def values(l, s):
                n = l * STEPS + s
                t, hg = place(l, s)
                pe.wait_ge(pt_moved, turned(l, s))
                if n:
                    pe.wait_ge(pv_moved, n)
                if l == 1:
                    pe.wait_ge(proj_free, G0[l] + 3 * (s // 4) + 3)
                    if s // 4:
                        pe.wait_ge(ot_rest, 2 * (s // 4))
                for j in range(2):
                    for b in range(t + 1):
                        flags = dict(start=(b == 0), stop=(b == t))
                        if l == 0:
                            last = pe.matmul(ps[HD * j:HD * j + HD, 7, 0:2 * P],
                                             vn[:, 0, b, (hg // 2) * HD:(hg // 2 + 1) * HD],
                                             pT[:, s % 2, b, 2 * j * P:2 * (j + 1) * P], **flags)
                        else:
                            h = 2 * (s % 2) + j
                            last = pe.matmul(ps[:, 7, j * VD:(j + 1) * VD],
                                             pT[:, s % 2, 0, (2 * b + j) * P:(2 * b + j + 1) * P],
                                             vn[:, (s // 4) % 2, b, h * VD:(h + 1) * VD], **flags)
                last.then_inc(pv_done, 1)

            def unit(u):
                pe.wait_ge(sub_done, u + 1)
                pe.wait_ge(pv_moved, STEPS + 4 * (u // T + 1))
                if u:
                    pe.wait_ge(ot_rest, u)
                for k in range(4):
                    last = pe.transpose(ps[:, 7, k * P:(k + 1) * P], orow[:, u % 2, k * P:(k + 1) * P], ident[:])
                last.then_inc(ot_done, 1)

            def route_products(l, j):
                pe.wait_ge(proj_free, G0[l] + QKV[l] + 4 + j + 1)
                if j >= 2:
                    pe.wait_ge(rt_moved, len(UNITS) * l + T * (j - 1))
                for t in range(T):
                    for b in range(BPG):
                        last = pe.matmul(ps[:, 4 + 2 * (j % 2) + t, b * P:(b + 1) * P],
                                         pqT[:, j % 2, b, t * P:(t + 1) * P], skT[:, 4 * j + b, :],
                                         start=True, stop=True)
                    last.then_inc(rt_done, 1)

            def spread_weights(l, t):
                pe.wait_ge(picks_ready, T * l + t + 1)
                for n, rows in enumerate((pickf[:, 0, :], pickf[:, 1, :], act[:, t, :])):
                    last = pe.transpose(ps[:, 4, n * P:(n + 1) * P], rows, ident[:])
                last.then_inc(pickT_done, 1)
                g0 = TB * (T * l + t)
                with pe.Fori(0, TB // 2) as it:
                    for buf in range(2):
                        for half in range(2):
                            if half == 0:
                                pe.wait_ge(hot2_ready, it * 2 + g0 + buf + 1)
                            pe.wait_ge(hot1_weighed, it * 4 + 2 * (g0 + buf) + half + 1)
                            pe.wait_ge(spread_moved, it * 4 + 2 * (g0 + buf) + half + 1)
                            for q in range(4):
                                last = pe.matmul(ps[:, 4 + half, q * P:(q + 1) * P],
                                                 onehot[:, buf, 0, 4 * half + q, :],
                                                 onehot[:, buf, 1, 4 * half + q, :], start=True, stop=True)
                            last.then_inc(spread_done, 1)

            def all_experts(l):
                pe.wait_ge(spread_moved, 2 * TB * T * (l + 1) + 2)

                def expert_block(r, at_, it, first=False):
                    pe.wait_ge(vblk_in[r], it * 16 + 16 * (l * (NKEYS // VRING) + 1))
                    for c in range(VB):
                        last = pe.matmul(ps[:, c // 2, (c % 2) * T * P:(c % 2 + 1) * T * P],
                                         vblk[:, r, c * P:(c + 1) * P], spread[:, :, at_, :],
                                         start=first and c % 2 == 0, stop=False,
                                         skip_group_check=True)
                    last.then_inc(vblk_used, 1)

                for r in range(VRING):
                    expert_block(r, slice(r, r + 1), 0, first=(r == 0))
                with pe.Fori(1, NKEYS // VRING) as it:
                    for r in range(VRING):
                        expert_block(r, bass.ds(it * VRING + r, 1), it)
                pe.wait_ge(vout_moved, 4 * (l + 1))
                for t in range(T):
                    pe.wait_ge(gathered, T * l + t + 1)
                    for c in range(VB):
                        last = pe.transpose(vsum(t)[:, c * P:(c + 1) * P], vout[:, c, t * P:(t + 1) * P], ident[:])
                    last.then_inc(vout_turned, 1)

            pe.sem_inc(spread_done, 4)
            pe.sem_inc(vblk_used, VRING)
            for l in range(DEPTH):
                transpose_x(2 * l)
                for i in range(len(STREAM[l])):
                    if i == WQ_SLOT[l]:
                        subkeys(l)
                        transpose_x(2 * l + 1)
                    s3, s2, s0 = step_at(l, i - 3), step_at(l, i - 2), step_at(l, i)
                    if s3 is not None:
                        values(l, s3)
                    for u in unit_at(l, i):
                        unit(u)
                    if s2 is not None:
                        turn(l, s2, 0)
                    if STREAM[l][i][0] == "wo":
                        if l == 0:
                            pe.wait_ge(pv_moved, 4 * (STREAM[l][i][2] + 1))
                        else:
                            pe.wait_ge(ot_rest, T * (STREAM[l][i][2] + 1))
                    half_chunk(l, i, 0)
                    if s2 is not None and l == 0 and place(l, s2)[0]:
                        turn(l, s2, 1)
                    if s0 is not None:
                        scores(l, s0)
                    j = i - WQ_SLOT[l]
                    if j > 0 and j % CH == 0:
                        route_products(l, j // CH - 1)
                    half_chunk(l, i, 1)
                route_products(l, PH // 2 - 1)
                for t in range(T):
                    spread_weights(l, t)
                all_experts(l)

        @block.vector
        def _(v):
            own = [0]

            def step(ins):
                ins.then_inc(dve_step, 1)
                own[0] += 1
                v.wait_ge(dve_step, own[0])

            v.sem_inc(slot_free, RING)
            v.sem_inc(vslot_free, VRING)
            v.sem_inc(vrow_begun, 1)
            v.sem_inc(dots_kept, 1)

            def low_part(l, i):
                c = C0[l] + i
                v.wait_ge(hi_done, c + 1)
                if c >= 2:
                    v.wait_ge(w_used, c - 1)
                v.tensor_tensor(w_lo[:, c % 2, POOL_KK:KK, :], raw[:, c % 2, POOL_KK:KK, :],
                                w_hi[:, c % 2, POOL_KK:KK, :].bitcast(F32), ALU.subtract).then_inc(lo_dve, 1)

            def rest_xT(n):
                for t in range(T):
                    for b in range(4):
                        v.wait_ge(xT_top, (n * T + t) * 4 + b + 1)
                        at_ = (slice(None), slice(4 * b, 4 * b + 4), slice(t * P, (t + 1) * P))
                        v.tensor_tensor(xT_lo[at_], ps[:, x_bank(n, t) + b, :].rearrange("p (k n) -> p k n", n=P),
                                        xT_hi[at_].bitcast(F32), ALU.subtract).then_inc(xT_rest, 1)

            def layer_norm(n0, gb):
                for t in range(T):
                    step(v.bn_aggr(mv[:, t, 0:2], stats[:, t].rearrange("p a b -> p (a b)")))
                    v.tensor_scalar(mv[:, t, 1:2], mv[:, t, 1:2], LN_EPS, None, ALU.add).then_inc(ln_var, 1)
                for t in range(T):
                    v.wait_ge(ln_root, n0 + t + 1)
                    step(v.reciprocal(mv[:, t, 3:4], mv[:, t, 2:3]))
                    v.tensor_scalar(mv[:, t, 4:5], mv[:, t, 0:1], mv[:, t, 3:4], -1.0, ALU.mult, ALU.mult
                                    ).then_inc(ln_recip, 1)
                v.wait_ge(gb_in, 32 * (n0 // T + 1))
                for t in range(T):
                    xs = xt[:, t, 0:POOL_FROM]
                    step(v.scalar_tensor_tensor(out=xs, in0=xs, scalar=mv[:, t, 0:1], in1=gb[:, 0, 0:POOL_FROM],
                                                op0=ALU.subtract, op1=ALU.mult))
                    v.scalar_tensor_tensor(out=xs, in0=xs, scalar=mv[:, t, 3:4], in1=gb[:, 1, 0:POOL_FROM],
                                           op0=ALU.mult, op1=ALU.add).then_inc(ln_done, 1)

            def residual(l, g):
                G, c0 = G0[l] + g, (g - QKV[l]) * GROUP
                v.wait_ge(w_used, group_done(l, g))
                for t in range(T):
                    xs = xt[:, t, c0:c0 + GROUP]
                    last = v.scalar_tensor_tensor(out=xs, in0=xs, scalar=ALPHA, in1=ps[:, 2 * (G % 2) + t, :],
                                                  op0=ALU.mult, op1=ALU.add)
                last.then_inc(proj_free, 1)
                v.wait_ge(proj_free, G + 1)
                for t in range(T):
                    last = v.bn_stats(stats[:, t, g - QKV[l], :], xt[:, t, c0:c0 + GROUP])
                step(last)

            def bias(l, s):
                n = l * STEPS + s
                t, hg = place(l, s)
                w = P * (t + 1)
                v.wait_ge(sc_done, n + 1)
                if s >= 3:
                    v.wait_ge(pt_done, turned(l, s - 3))
                for m in range(4):
                    slope = slopes[0][4 * hg + m] if l == 0 else slopes[1][2 * hg + m // 2]
                    last = v.scalar_tensor_tensor(
                        out=prob[:, s % 3, m, 0:w], in0=mask[:, l, 2 * P - w:2 * P], scalar=slope / SCALE,
                        in1=ps[:, 4 + m % 2, (m // 2) * 256:(m // 2) * 256 + w], op0=ALU.mult, op1=ALU.add)
                step(last)
                mx_s, nm_s, sk_s = mx[:, s % 2, :], nm[:, s % 2, :], sk[:, s % 2, :]
                step(v.tensor_reduce(mx_s, prob[:, s % 3, :, 0:w], AX_X, ALU.max))
                if l == 0:
                    sinks = sink8[:, 4 * hg:4 * hg + 4]
                    step(v.tensor_tensor(mx_s, mx_s, sinks, ALU.max))
                    v.tensor_tensor(sk_s, sinks, mx_s, ALU.subtract)
                    step(v.tensor_scalar(nm_s, mx_s, -SCALE, None, ALU.mult))
                    v.tensor_scalar(sk_s, sk_s, SCALE, None, ALU.mult).then_inc(sc_ready, 1)
                else:
                    v.tensor_scalar(nm_s, mx_s, -SCALE, None, ALU.mult).then_inc(sc_ready, 1)

            def norm(l, s):
                t, _ = place(l, s)
                w = P * (t + 1)
                rd_s, p = rd[:, s % 2, :], prob[:, s % 3]
                v.wait_ge(sc_exp, l * STEPS + s + 1)
                if l == 0:
                    step(v.tensor_tensor(rd_s, rs[:, s % 2, :], sk[:, s % 2, :], ALU.add))
                    step(v.reciprocal(rd_s, rd_s))
                    for m in range(4):
                        last = v.tensor_scalar(p[:, m, 0:w], p[:, m, 0:w], rd_s[:, m:m + 1], None, ALU.mult)
                else:
                    step(v.reciprocal(rd_s, rs[:, s % 2, :]))
                    step(v.tensor_scalar(rd_s[:, 1:4:2], rd_s[:, 1:4:2], sm[:, 5:6], None, ALU.mult))
                    for m in (1, 3):
                        last = v.tensor_scalar(p[:, m, 0:w], p[:, m, 0:w], rd_s[:, m:m + 1], None, ALU.mult)
                    step(last)
                    for m in (0, 2):
                        last = v.scalar_tensor_tensor(out=p[:, m, 0:w], in0=p[:, m, 0:w], scalar=rd_s[:, m:m + 1],
                                                      in1=p[:, m + 1, 0:w], op0=ALU.mult, op1=ALU.add)
                last.then_inc(prob_ready, 1)

            def move(l, s):
                t, hg = place(l, s)
                if l == 0:
                    v.wait_ge(pv_top, s + 1)
                    at_ = (slice(None), slice(2 * hg, 2 * hg + 2), slice(t * P, (t + 1) * P))
                    v.tensor_tensor(oT_lo[at_], ps[:, 7, 0:2 * P].rearrange("p (j q) -> p j q", q=P),
                                    oT_hi[at_].bitcast(F32), ALU.subtract).then_inc(pv_moved, 1)
                else:
                    u = s // 2
                    v.wait_ge(pv_done, STEPS + s + 1)
                    if s % 2 == 0 and u >= 2:
                        v.wait_ge(ot_done, u - 1)
                    v.tensor_copy(orow[:, u % 2, (s % 2) * 2 * VD:(s % 2 + 1) * 2 * VD], ps[:, 7, 0:2 * VD]
                                  ).then_inc(pv_moved, 1)

            def sub_norm(l, u):
                li = 0.8 - 0.6 * math.exp(-0.3 * l)
                o = orow[:, u % 2, :]
                o3 = o.rearrange("p (h e) -> p h e", e=VD)
                v.wait_ge(pv_moved, STEPS + 2 * u + 2)
                step(v.tensor_tensor(osq[:], o, o, ALU.mult))
                step(v.tensor_reduce(sq[:, 0, :], osq[:].rearrange("p (h e) -> p h e", e=VD), AX_X, ALU.add))
                v.tensor_scalar(sq[:, 0, :], sq[:, 0, :], 1.0 / VD, LN_EPS, ALU.mult, ALU.add).then_inc(sub_sq, 1)
                v.wait_ge(sub_rt, u + 1)
                step(v.reciprocal(sq[:, 2, :], sq[:, 1, :]))
                step(v.tensor_scalar(sq[:, 2, :], sq[:, 2, :], 1.0 - li, None, ALU.mult))
                step(v.tensor_tensor(o3, o3, sq[:, 2, :].unsqueeze(2).broadcast_to([P, 4, VD]), ALU.mult))
                v.tensor_tensor(o3, o3, subg[:].unsqueeze(1).broadcast_to([P, 4, VD]), ALU.mult).then_inc(sub_done, 1)

            def unit_rest(u):
                h, t = u // T, u % T
                v.wait_ge(ot_top, u + 1)
                at_ = (slice(None), slice(4 * h, 4 * h + 4), slice(t * P, (t + 1) * P))
                v.tensor_tensor(oT_lo[at_], ps[:, 7, :].rearrange("p (k n) -> p k n", n=P),
                                oT_hi[at_].bitcast(F32), ALU.subtract).then_inc(ot_rest, 1)

            def top16(n, vals, out_v, out_i):
                for half in range(2):
                    eight = slice(8 * half, 8 * half + 8)
                    for j in range(n):
                        last = v.max(out_v[:, j, eight], vals[:, j, :])
                    step(last)
                    for j in range(n):
                        last = v.max_index(out_i[:, j, eight], out_v[:, j, eight], vals[:, j, :])
                    step(last)
                    if half == 0:
                        for j in range(n):
                            last = v.match_replace(vals[:, j, :], out_v[:, j, eight], vals[:, j, :], LOWEST)
                        step(last)

            def route(l, n, heads=range(2)):
                j, t = UNITS[n]
                H, h0 = len(heads), heads[0]
                scores = sc[:, j, t, 2 * NKEYS * h0:2 * NKEYS * (h0 + H)]
                top_, topi_, topf_ = top[:, 0:2 * H], topi[:, 0:2 * H], topf[:, 0:2 * H]
                cand_, best_, pos_, posf_ = cand[:, 0:H], best[:, 0:H], pos[:, :, 0:H * TOPK], posf[:, :, 0:H * TOPK]
                hot_, key_ = hot[:, 0:H * TOPK], key[:, :, 0:H * TOPK]
                v.wait_ge(rt_moved, len(UNITS) * l + T * j + t + 1)
                top16(2 * H, scores.rearrange("p (c k) -> p c k", k=NKEYS), top_, topi_)
                v.tensor_copy(topf_, topi_)
                halves = top_.rearrange("p (h c) k -> p h c k", c=2)
                step(v.tensor_tensor(cand_.rearrange("p h (i j) -> p h i j", j=TOPK),
                                     halves[:, :, 0, :].unsqueeze(3).broadcast_to([P, H, TOPK, TOPK]),
                                     halves[:, :, 1, :].unsqueeze(2).broadcast_to([P, H, TOPK, TOPK]), ALU.add))
                top16(H, cand_, best_, pos_[:, 0, :].rearrange("p (h k) -> p h k", h=H))
                at_ = slice(TOPK * (2 * j + h0), TOPK * (2 * j + h0 + H))
                v.tensor_tensor(gate[:, t, at_].rearrange("p (h k) -> p h k", h=H), best_,
                                best_[:, :, 0:1].broadcast_to([P, H, TOPK]), ALU.subtract).then_inc(gate_sub, 1)
                v.tensor_scalar(pos_[:, 1, :], pos_[:, 0, :], 4, None, ALU.logical_shift_right)
                step(v.tensor_scalar(pos_[:, 2, :], pos_[:, 0, :], TOPK - 1, None, ALU.bitwise_and))
                step(v.tensor_copy(posf_, pos_[:, 1:3, :]))
                keys = topf_.rearrange("p (h c) k -> p h c k", c=2)
                if t and j:
                    v.wait_ge(pickT_done, T * l + 1)
                for c in range(2):
                    step(v.tensor_tensor(hot_, posf_[:, c, :].unsqueeze(2).broadcast_to([P, H * TOPK, TOPK]),
                                         iota16[:].unsqueeze(1).broadcast_to([P, H * TOPK, TOPK]), ALU.is_equal))
                    h4 = hot_.rearrange("p (h n) k -> p h n k", h=H)
                    step(v.tensor_tensor(h4, h4, keys[:, :, c, :].unsqueeze(2).broadcast_to([P, H, TOPK, TOPK]),
                                         ALU.mult))
                    step(v.tensor_reduce(key_[:, c, :], hot_, AX_X, ALU.add))
                if l:
                    step(v.tensor_scalar(key_[:, 1, :], key_[:, 1, :], float(l * NKEYS * NKEYS), None, ALU.add))
                v.scalar_tensor_tensor(out=idx[:, t, at_], in0=key_[:, 0, :], scalar=float(NKEYS),
                                       in1=key_[:, 1, :], op0=ALU.mult, op1=ALU.add).then_inc(routed, 1)
                v.wait_ge(routed, ROUTES * l + n + 1 + (n > 0 or h0 + H == 2))

            def dot_batch(t, col, batch, it=0, stride=0):
                v.wait_ge(dots_kept, it * stride + batch + 1)
                for r in range(RING):
                    v.wait_ge(rows_in[r], it * (16 * stride) + 16 * (batch + 1))
                    v.tensor_tensor_reduce(ring[:, r, :], ring[:, r, :], xt[:, t, :], 1.0, 0.0, ALU.mult, ALU.add,
                                           act8[:, r:r + 1]).then_inc(slot_free, 1)
                v.wait_ge(slot_free, it * (stride * RING) + (batch + 2) * RING)
                v.tensor_copy(act[:, t, bass.ds(it * (stride * RING) + col, RING)], act8[:]).then_inc(dots_kept, 1)

            def weigh(l, t):
                if T * l + t:
                    v.wait_ge(pickT_done, T * l + t)
                v.tensor_scalar(pick[:, 1, :], idx[:, t, :], NKEYS - 1, None, ALU.bitwise_and)
                step(v.tensor_scalar(pick[:, 0, :], idx[:, t, :], 7, None, ALU.logical_shift_right))
                step(v.tensor_scalar(pick[:, 0, :], pick[:, 0, :], NKEYS - 1, None, ALU.bitwise_and))
                step(v.tensor_copy(pickf[:], pick[:]))
                gate_h = gate[:, t, :].rearrange("p (h k) -> p h k", h=PH)
                v.wait_ge(gate_exp, T * l + t + 1)
                step(v.tensor_reduce(gsum[:, 0, :], gate_h, AX_X, ALU.add))
                step(v.reciprocal(gsum[:, 1, :], gsum[:, 0, :]))
                step(v.tensor_tensor(gate_h, gate_h, gsum[:, 1, :].unsqueeze(2).broadcast_to([P, PH, TOPK]), ALU.mult))
                if t:
                    step(v.memset(vsum(0), 0.0))
                    add_rows(l, 0, 0, VRING, 0, 0)
                v.wait_ge(gelu_done, T * l + t + 1)
                v.tensor_tensor(act[:, t, :], gate[:, t, :], act[:, t, :], ALU.mult).then_inc(picks_ready, 1)

            def one_hots(l, t, tok, buf, g, it, stride):
                v.wait_ge(spread_done, it * (2 * stride) + 2 * g + 2)
                v.wait_ge(pickT_moved, T * l + t + 1)
                keys = pickT[:, 0, bass.ds(it * (stride * SPREAD) + tok, SPREAD)]
                v.tensor_tensor(onehot[:, buf, 1], keys.unsqueeze(2).broadcast_to([P, SPREAD, P]),
                                iota_keys[:].unsqueeze(1).broadcast_to([P, SPREAD, P]), ALU.is_equal
                                ).then_inc(hot1_ready, 1)

            def add_rows(l, t, col, n, it, stride):
                acc = vsum(t)
                job = l * JOBS + t * PICKS + col
                for r in range(n):
                    weight = act[:, t, bass.ds(it * stride + col + r, 1)]
                    v.wait_ge(vrow_begun, it * stride + job + r + 1)
                    v.wait_ge(vrows_in[r % VRING], it * (16 * stride // VRING) + 16 * ((job + r) // VRING + 1))
                    v.scalar_tensor_tensor(out=acc[:, 0:GROUP], in0=vring[:, r % VRING, 0:GROUP], scalar=weight,
                                           in1=acc[:, 0:GROUP], op0=ALU.mult, op1=ALU.add).then_inc(vrow_begun, 1)
                    v.wait_ge(vslot_free, it * stride + job + r + VRING)
                    v.scalar_tensor_tensor(out=acc[:, GROUP:VG], in0=vring[:, r % VRING, GROUP:VG], scalar=weight,
                                           in1=acc[:, GROUP:VG], op0=ALU.mult, op1=ALU.add).then_inc(vslot_free, 1)

            def add_half(l, t, half):
                xs = xt[:, t, half * VG:(half + 1) * VG]
                if half == 0:
                    v.wait_ge(vrow_begun, l * JOBS + (t + 1) * PICKS + 1)
                    v.wait_ge(vslot_free, l * JOBS + (t + 1) * PICKS + VRING)
                ins = v.scalar_tensor_tensor(out=xs, in0=xs, scalar=ALPHA, in1=vsum(t), op0=ALU.mult, op1=ALU.add)
                if half == 0:
                    ins.then_inc(gathered, 1)
                    v.wait_ge(gathered, T * l + t + 1)
                else:
                    step(ins)
                for c in range(2 * half, 2 * half + 2):
                    last = v.bn_stats(stats[:, t, c, :], xt[:, t, c * GROUP:(c + 1) * GROUP])
                step(last)

            v.wait_ge(small_in, 6 * 16)
            step(v.tensor_scalar(sink8[:], sink8[:], 1.0 / SCALE, None, ALU.mult))
            for j in range(2):
                v.tensor_tensor_reduce(lamv[:, 2 * j, :], lamv[:, 2 * j, :], lamv[:, 2 * j + 1, :], 1.0, 0.0, ALU.mult,
                                       ALU.add, sm[:, j:j + 1]).then_inc(lam_dot, 1)
            v.wait_ge(const_pool, 10)
            for l in range(DEPTH):
                if l == 1:
                    v.wait_ge(lam_exp, 1)
                    step(v.tensor_tensor(sm[:, 4:5], sm[:, 3:4], sm[:, 2:3], ALU.subtract))
                    step(v.tensor_scalar(sm[:, 5:6], sm[:, 4:5], -(0.8 - 0.6 * math.exp(-0.3 * l)), None, ALU.add))
                rest_xT(2 * l)
                low_part(l, 0)
                for i in range(WQ_SLOT[l]):
                    for g in finished(l, i):
                        if g >= QKV[l]:
                            residual(l, g)
                    low_part(l, i + 1)
                    s3, s1, s0 = step_at(l, i - 3), step_at(l, i - 1), step_at(l, i)
                    if s1 is not None:
                        norm(l, s1)
                    if s3 is not None:
                        move(l, s3)
                        if l == 1 and s3 % 2 == 1:
                            sub_norm(l, s3 // 2)
                    for u in unit_at(l, i):
                        unit_rest(u)
                    if s0 is not None:
                        bias(l, s0)
                residual(l, QKV[l] + 3)
                layer_norm(2 * T * l, gb1)
                rest_xT(2 * l + 1)
                for i in range(WQ_SLOT[l] + 1, WQ_SLOT[l] + CH):
                    low_part(l, i)
                b0 = l * BATCHES
                route(l, 0, range(0, 1))
                route(l, 0, range(1, 2))
                for m in range(T):
                    ln_finished(v, 2 * T * l + m)
                for b in range(UB):
                    dot_batch(0, b * RING, b0 + b)
                    if b == 0:
                        route(l, 1)
                route(l, 2)
                for n, (j, t) in enumerate(UNITS[1:], 1):
                    with v.Fori(0, UB // 2) as it:
                        for half in range(2):
                            dot_batch(t, 2 * TOPK * j + half * RING, b0 + n * UB + half, it, 2)
                            if t:
                                b = j * UB + half
                                one_hots(l, 0, b * SPREAD, half, T * TB * l + b, it, 2)
                    if j == PH // 2 - 1:
                        weigh(l, t)
                    if n + 2 < len(UNITS):
                        route(l, n + 2)
                with v.Fori(0, TB // 2) as it:
                    for half in range(2):
                        one_hots(l, 1, half * SPREAD, half, TB * (T * l + 1) + half, it, 2)
                        add_rows(l, 0, (half + 1) * VRING, VRING, it, 2 * VRING)
                with v.Fori(0, (PICKS - (TB + 1) * VRING) // VRING) as it:
                    add_rows(l, 0, (TB + 1) * VRING, VRING, it, VRING)
                add_half(l, 0, 0)
                v.wait_ge(spread_moved, 2 * TB * T * (l + 1) + 2)
                step(v.memset(vsum(1), 0.0))
                with v.Fori(0, TB) as it:
                    add_rows(l, 1, 0, RING, it, RING)
                add_half(l, 1, 0)
                for t in range(T):
                    v.wait_ge(vout_turned, T * l + t + 1)
                    add_half(l, t, 1)
                layer_norm(2 * T * l + T, gb2)


_INS = ['x', 'a_w_qkv', 'a_sinks', 'a_w_o', 'b_w_qkv', 'b_lambda_q1', 'b_lambda_k1', 'b_lambda_q2', 'b_lambda_k2',
        'b_subln_g', 'b_w_o', 'ln1_g', 'ln1_b', 'ln2_g', 'ln2_b', 'peer_w_q', 'peer_subkeys', 'peer_u', 'peer_v']


def kernel(**inputs):
    import numpy as _np
    import concourse.bacc as _bacc
    from concourse import mybir as _mybir
    from concourse.bass_utils import run_bass_kernel_spmd as _run

    nc = _bacc.Bacc("TRN2", target_bir_lowering=False, num_devices=1)
    arrays, args = {}, []
    for name in _INS:
        a = _np.ascontiguousarray(inputs[name])
        arrays[f"in_{name}_dram"] = a
        args.append(nc.dram_tensor(f"in_{name}_dram", a.shape, _mybir.dt.from_np(a.dtype), kind="ExternalInput").ap())
    shape = inputs["x"].shape
    args.append(nc.dram_tensor("out_0_dram", shape, _mybir.dt.from_np(_np.dtype("float32")),
                               kind="ExternalOutput").ap())
    decoder_trunk(nc, *args)
    r = _run(nc, [arrays], core_ids=[0])
    return r.results[0]["out_0_dram"]
```
